# Optimizing a Trainium2 kernel written in Bass

```python
import math
import jax, jax.numpy as jnp
from jax import lax
import numpy as np

D_MODEL = 2048
BATCH = 1
SEQ = 128
DEPTH = 1
DEC_BATCH = 1
DEC_SEQ = 512
PAST_LEN = 256

GRID_W = 64
Q_BLOCK = 128
ROPE_THETA = 10000.0
EPS = 1e-6
H_A = 8
DK_A = 64
DV_A = 2 * DK_A
H_B = 8
KV_B = 2
DH_B = 128
G_B = H_B // KV_B
A_Q = H_A * 2 * DK_A
A_K = H_A * 2 * DK_A
A_V = H_A * DV_A
A_G = H_A * DV_A
B_Q = H_B * DH_B
B_K = KV_B * DH_B
B_V = KV_B * DH_B
B_G = H_B * DH_B
D_IN = A_Q + A_K + A_V + A_G + B_Q + B_K + B_V + B_G
D_MIX = A_V + B_Q
SPLIT_POINTS = [int(s) for s in np.cumsum([A_Q, A_K, A_V, A_G, B_Q, B_K, B_V])]

kernel_name = "hymba_diff_gqa_diffusion_step"

def rms_norm(x, g):
    xf = x.astype(jnp.float32)
    y = xf * lax.rsqrt(jnp.mean(xf * xf, axis=-1, keepdims=True) + EPS)
    return (y * g.astype(jnp.float32)).astype(x.dtype)

def adaln(cond, w_ada_l, b_ada_l):
    mod = jax.nn.silu(cond) @ w_ada_l + b_ada_l
    return jnp.split(mod, 3, axis=-1)

def axial_rope(n_tok, rot_dim):
    n_rows = n_tok // GRID_W
    rows = jnp.repeat(jnp.arange(n_rows, dtype=jnp.float32), GRID_W)
    cols = jnp.tile(jnp.arange(GRID_W, dtype=jnp.float32), n_rows)
    quarter = rot_dim // 4
    inv_freq = 1.0 / (ROPE_THETA ** (jnp.arange(quarter, dtype=jnp.float32) / quarter))
    ang = jnp.concatenate([rows[:, None] * inv_freq, cols[:, None] * inv_freq], axis=-1)
    return jnp.cos(ang), jnp.sin(ang)

def apply_rope(x, cos, sin):
    shape = (1, cos.shape[0]) + (1,) * (x.ndim - 3) + (cos.shape[1],)
    cos = cos.reshape(shape)
    sin = sin.reshape(shape)
    xf = x.astype(jnp.float32)
    x1, x2 = jnp.split(xf, 2, axis=-1)
    out = jnp.concatenate([x1 * cos - x2 * sin, x1 * sin + x2 * cos], axis=-1)
    return out.astype(x.dtype)

def sweep_query_blocks(attend, q):
    b, lq = q.shape[:2]
    nb = lq // Q_BLOCK
    qb = jnp.moveaxis(q.reshape((b, nb, Q_BLOCK) + q.shape[2:]), 1, 0)
    out = lax.map(attend, qb)
    out = jnp.moveaxis(out, 0, 1)
    return out.reshape((b, lq) + out.shape[3:])

def diff_attention(q, k, v, lam):
    scale = 1.0 / math.sqrt(DK_A)

    def attend(qb):
        s = jnp.einsum('bqhcd,bshcd->bhcqs', qb, k).astype(jnp.float32) * scale
        p = jax.nn.softmax(s, axis=-1)
        p = p[:, :, 0] - lam[None, :, None, None] * p[:, :, 1]
        return jnp.einsum('bhqs,bshe->bqhe', p.astype(v.dtype), v)

    return sweep_query_blocks(attend, q)

def gqa_attention(q, k, v):
    b, lq = q.shape[:2]
    q = q.reshape(b, lq, KV_B, G_B, DH_B)
    scale = 1.0 / math.sqrt(DH_B)

    def attend(qb):
        s = jnp.einsum('bqkgd,bskd->bkgqs', qb, k).astype(jnp.float32) * scale
        p = jax.nn.softmax(s, axis=-1)
        return jnp.einsum('bkgqs,bskd->bqkgd', p.astype(v.dtype), v)

    out = sweep_query_blocks(attend, q)
    return out.reshape(b, lq, H_B, DH_B)

def mixer_inputs(h, w_in_l, q_norm_l, k_norm_l):
    b, n = h.shape[:2]
    z = h @ w_in_l
    qa, ka, va, ga, qb, kb, vb, gb = jnp.split(z, SPLIT_POINTS, axis=-1)
    qa = qa.reshape(b, n, H_A, 2, DK_A)
    ka = ka.reshape(b, n, H_A, 2, DK_A)
    va = va.reshape(b, n, H_A, DV_A)
    qb = rms_norm(qb.reshape(b, n, H_B, DH_B), q_norm_l)
    kb = rms_norm(kb.reshape(b, n, KV_B, DH_B), k_norm_l)
    vb = vb.reshape(b, n, KV_B, DH_B)
    return qa, ka, va, ga, qb, kb, vb, gb

def mixer_outputs(oa, ob, ga, gb, subln_l, lam_init, w_out_l):
    b, n = oa.shape[:2]
    oa = rms_norm(oa, subln_l) * (1.0 - lam_init)
    o = jnp.concatenate([oa.reshape(b, n, A_V) * jax.nn.silu(ga),
                         ob.reshape(b, n, B_Q) * jax.nn.silu(gb)], axis=-1)
    return o @ w_out_l

def diff_lambda(lq1, lk1, lq2, lk2, lam_init):
    f = jnp.float32
    return (jnp.exp(jnp.sum(lq1.astype(f) * lk1.astype(f), axis=-1))
            - jnp.exp(jnp.sum(lq2.astype(f) * lk2.astype(f), axis=-1)) + lam_init)

def setup_inputs(seed: int = 0) -> dict:
    key = jax.random.key(seed)
    ks = jax.random.split(key, 24)
    f = jnp.float32
    nrm = lambda k, s: jax.random.normal(k, s, f)
    d = D_MODEL
    return {
        "x_prompt": nrm(ks[0], (BATCH, SEQ, d)),
        "x_sample": nrm(ks[1], (DEC_BATCH, DEC_SEQ, d)),
        "cache_diff_k": nrm(ks[2], (DEC_BATCH, DEPTH, PAST_LEN, H_A, 2 * DK_A)),
        "cache_diff_v": nrm(ks[3], (DEC_BATCH, DEPTH, PAST_LEN, H_A, DV_A)),
        "cache_gqa_k": nrm(ks[4], (DEC_BATCH, DEPTH, PAST_LEN, KV_B, DH_B)),
        "cache_gqa_v": nrm(ks[5], (DEC_BATCH, DEPTH, PAST_LEN, KV_B, DH_B)),
        "c": nrm(ks[6], (DEC_BATCH, d)),
        "c_ctx": nrm(ks[7], (d,)),
        "w_ada": nrm(ks[8], (DEPTH, d, 3 * d)) * (0.5 * d ** -0.5),
        "b_ada": nrm(ks[9], (DEPTH, 3 * d)) * 0.02,
        "g_norm": 1.0 + 0.05 * nrm(ks[10], (DEPTH, d)),
        "w_in": nrm(ks[11], (DEPTH, d, D_IN)) * d ** -0.5,
        "lam_q1": nrm(ks[12], (DEPTH, H_A, DK_A)) * 0.1,
        "lam_k1": nrm(ks[13], (DEPTH, H_A, DK_A)) * 0.1,
        "lam_q2": nrm(ks[14], (DEPTH, H_A, DK_A)) * 0.1,
        "lam_k2": nrm(ks[15], (DEPTH, H_A, DK_A)) * 0.1,
        "subln_g": 1.0 + 0.05 * nrm(ks[16], (DEPTH, DV_A)),
        "q_norm_g": 1.0 + 0.05 * nrm(ks[17], (DEPTH, DH_B)),
        "k_norm_g": 1.0 + 0.05 * nrm(ks[18], (DEPTH, DH_B)),
        "w_out": nrm(ks[19], (DEPTH, D_MIX, d)) * D_MIX ** -0.5,
        "g_final": 1.0 + 0.05 * nrm(ks[20], (d,)),
    }

def reference(x_prompt, x_sample, cache_diff_k, cache_diff_v, cache_gqa_k, cache_gqa_v,
              c, c_ctx, w_ada, b_ada, g_norm, w_in, lam_q1, lam_k1, lam_q2, lam_k2,
              subln_g, q_norm_g, k_norm_g, w_out, g_final):
    xp = x_prompt
    xs = x_sample
    bp, n_ctx = xp.shape[:2]
    bs, n_lat = xs.shape[:2]
    n_past = cache_diff_k.shape[2]
    cos_a, sin_a = axial_rope(n_lat, DK_A)
    cos_b, sin_b = axial_rope(n_lat, DH_B)
    st_dk, st_dv, st_gk, st_gv = [], [], [], []
    for l in range(DEPTH):
        lam_init = 0.8 - 0.6 * math.exp(-0.3 * l)
        lam = diff_lambda(lam_q1[l], lam_k1[l], lam_q2[l], lam_k2[l], lam_init)

        shift, scale, gate = adaln(c_ctx[None, None, :], w_ada[l], b_ada[l])
        h = rms_norm(xp, g_norm[l]) * (1.0 + scale) + shift
        qa, ka, va, ga, qb, kb, vb, gb = mixer_inputs(h, w_in[l], q_norm_g[l], k_norm_g[l])
        oa = diff_attention(qa, ka, va, lam)
        ob = gqa_attention(qb, kb, vb)
        xp = xp + gate * mixer_outputs(oa, ob, ga, gb, subln_g[l], lam_init, w_out[l])
        st_dk.append(ka.reshape(bp, n_ctx, H_A, 2 * DK_A))
        st_dv.append(va)
        st_gk.append(kb)
        st_gv.append(vb)

        shift, scale, gate = adaln(c[:, None, :], w_ada[l], b_ada[l])
        h = rms_norm(xs, g_norm[l]) * (1.0 + scale) + shift
        qa, ka, va, ga, qb, kb, vb, gb = mixer_inputs(h, w_in[l], q_norm_g[l], k_norm_g[l])
        qa = apply_rope(qa, cos_a, sin_a)
        ka = apply_rope(ka, cos_a, sin_a)
        qb = apply_rope(qb, cos_b, sin_b)
        kb = apply_rope(kb, cos_b, sin_b)
        ka_all = jnp.concatenate([ka, cache_diff_k[:, l].reshape(bs, n_past, H_A, 2, DK_A)], axis=1)
        va_all = jnp.concatenate([va, cache_diff_v[:, l]], axis=1)
        kb_all = jnp.concatenate([kb, cache_gqa_k[:, l]], axis=1)
        vb_all = jnp.concatenate([vb, cache_gqa_v[:, l]], axis=1)
        oa = diff_attention(qa, ka_all, va_all, lam)
        ob = gqa_attention(qb, kb_all, vb_all)
        xs = xs + gate * mixer_outputs(oa, ob, ga, gb, subln_g[l], lam_init, w_out[l])

    y_prompt = rms_norm(xp, g_final)
    y_sample = rms_norm(xs, g_final)
    new_diff_k = jnp.stack(st_dk, axis=1)
    new_diff_v = jnp.stack(st_dv, axis=1)
    new_gqa_k = jnp.stack(st_gk, axis=1)
    new_gqa_v = jnp.stack(st_gv, axis=1)
    return (y_prompt, y_sample, new_diff_k, new_diff_v, new_gqa_k, new_gqa_v)


_drawn_inputs = setup_inputs


def setup_inputs(seed=0):
    import zlib

    import numpy as np

    out = dict(_drawn_inputs(seed))
    spreads = {}
    factors = {'cache_diff_k': 2.778,
     'cache_gqa_k': 8.0,
     'cache_gqa_v': 8.0,
     'lam_q1': 6.767,
     'lam_k1': 6.133,
     'lam_q2': 8.0,
     'lam_k2': 8.0,
     'subln_g': 8.0,
     'q_norm_g': 8.0}
    for name, (base, spread) in spreads.items():
        noise = np.random.default_rng([zlib.crc32(name.encode()), seed]).standard_normal(out[name].shape)
        drawn = base * np.exp(spread * noise) if base else spread * noise
        out[name] = __import__('jax').numpy.asarray(drawn.astype(out[name].dtype))
    for name, factor in factors.items():
        out[name] = (out[name] * factor).astype(out[name].dtype)
    return out
```

```python
import math
from contextlib import ExitStack

import numpy as np

import concourse.bass as bass
from concourse import mybir

F32 = mybir.dt.float32
F32R = mybir.dt.float32r
ALU = mybir.AluOpType
ACT = mybir.ActivationFunctionType
AX_X = mybir.AxisListType.X

P = 128
D_MODEL = 2048
KT = D_MODEL // P
TILES = 5
LAT = 4
PAST = 2
NKEY = (LAT + PAST) * P
H_A, DK_A = 8, 64
H_B, KV_B, DH = 8, 2, 128
NCOL = 512
LAM_INIT = 0.8 - 0.6 * math.exp(0.0)
EPS = 1e-6
GRID_W = 64
A_COLS = 4 * H_A * DH
QB0 = A_COLS
KB0 = QB0 + H_B * DH
GB0 = KB0 + 2 * KV_B * DH

KV_IT = H_A
G_IT = KV_IT + 1
OUT_IT = G_IT + H_B // 2
OUTS = D_MODEL // NCOL
ITS = OUT_IT + OUTS
RING = 3
W_RING = 4
W_AHEAD = 3
RAW_RING = 2
ADA_RING = 5
H_AHEAD = 2
GATE_SLOT = 4

STEPS = {
    1: [("O", -1)], 3: [("QK", 0)], 4: [("S", 0)], 5: [("S", 1)], 6: [("T", 0)], 7: [("V", 0), ("S", 2)],
    8: [("T", 1)], 9: [("V", 1), ("S", 3)], 10: [("T", 2)], 11: [("V", 2), ("S", 4)], 12: [("T", 3)],
    13: [("V", 3)], 14: [("T", 4)], 15: [("V", 4)],
}
LAST_STEPS = dict(STEPS)
LAST_STEPS[13] = [("V", 3), ("T", 4), ("V", 4), ("O", 0)]
LAST_STEPS[14] = LAST_STEPS[15] = []


def group_kind(a):
    return "D" if a < H_A else "KV" if a == KV_IT else "G"


def steps_at(it, s):
    out = []
    if it > OUT_IT:
        return out
    for kind, t in (LAST_STEPS if it == OUT_IT else STEPS).get(s, []):
        a = it - 1
        if kind == "O":
            a, t = a + t, 0
        if not 0 <= a < OUT_IT:
            continue
        if group_kind(a) == "KV" and kind != "QK":
            continue
        out.append((kind, a, t))
    return out


def banks_of(kind, a, t):
    g = group_kind(a)
    if kind == "QK":
        return 4 if g == "KV" else 3
    if kind == "S":
        return 4 if t else 2
    if kind == "T":
        return (2 if t else 1) * (2 if g == "G" and t else 1)
    if kind == "O":
        return 4 if g == "G" else 2
    return 1


def count_turns():
    turn, n = {}, 0
    for key, k in [("VEC", 1), ("SCALE", 1), ("SHIFT", 1), ("COLS", 2)]:
        turn[key] = n
        n += k
    for kt in range(KT):
        turn[("HT", kt)] = n
        n += 2
    for it in range(ITS):
        for s in range(KT):
            for step in steps_at(it, s):
                turn[step] = n
                n += banks_of(*step)
            if it == G_IT and s == GATE_SLOT:
                turn["GATE"] = n
                n += 1
    return turn


def gate_pieces(s):
    slots = KT - GATE_SLOT
    return range(2 * KT * (s - GATE_SLOT) // slots, 2 * KT * (s - GATE_SLOT + 1) // slots)


TURN = count_turns()


def build(nc, x_prompt, x_sample, cache_diff_k, cache_diff_v, cache_gqa_k, cache_gqa_v, c, c_ctx, w_ada,
          b_ada, g_norm, w_in, lam_q1, lam_k1, lam_q2, lam_k2, subln_g, q_norm_g, k_norm_g, w_out, g_final,
          ropes_a, ropes_b, y_prompt, y_sample, new_dk, new_dv, new_gk, new_gv):
    w_in2 = w_in[0]
    w_out2 = w_out[0]
    w_ada2 = w_ada[0]
    wa_v = w_in2[:, 0:A_COLS].rearrange("(k p) (s h c) -> h p k s c", p=P, s=4, h=H_A)
    w_v = w_in2.rearrange("(k p) n -> p k n", p=P)
    wo_v = w_out2.rearrange("(k p) n -> p k n", p=P)
    ada_v = w_ada2.rearrange("(k p) n -> k p n", p=P)
    xs_v = x_sample[0].rearrange("(t p) d -> p t d", p=P)
    dk_v = cache_diff_k[0, 0].rearrange("(j p) h d -> p j h d", p=P)
    dv_v = cache_diff_v[0, 0].rearrange("(j p) h d -> p j h d", p=P)
    gk_v = cache_gqa_k[0, 0].rearrange("(j p) h d -> p j h d", p=P)
    gv_v = cache_gqa_v[0, 0].rearrange("(j p) h d -> p j h d", p=P)
    o_spill = nc.dram_tensor("o_spill", (H_A + H_B, P, TILES * P), F32).ap()
    gate_rows = nc.dram_tensor("gate_rows", (2, D_MODEL), F32).ap()

    at = [(nc.sbuf_base + 31) // 32 * 32]

    def region(nbytes):
        start = at[0]
        at[0] += (nbytes + 31) // 32 * 32
        assert at[0] <= nc.sbuf_usable_end, (at[0], nc.sbuf_usable_end)
        return start

    def place(name, shape, dt, start):
        size = 4 * int(np.prod(shape[1:]))
        return nc.alloc_sbuf_tensor_at(name, list(shape), dt, offset=start), start + size

    def new(name, shape, dt=F32):
        return place(name, shape, dt, region(4 * int(np.prod(shape[1:]))))[0]

    xt_hi = new("xt_hi", [P, KT, TILES * P], F32R)
    xt_lo = new("xt_lo", [P, KT, TILES * P], F32R)
    w_hi = new("w_hi", [P, W_RING, NCOL], F32R)
    w_lo = new("w_lo", [P, W_RING, NCOL], F32R)
    w_raw = new("w_raw", [P, RAW_RING, 2, NCOL])
    r1 = region(4 * 12800)
    ada_raw, e = place("ada_raw", [P, ADA_RING, D_MODEL], F32, r1)
    lam_raw, e = place("lam_raw", [P, 4, H_A * DK_A], F32, e)
    vec_rows, e = place("vec_rows", [96, P], F32, e)
    cs_t, e = place("cs_t", [P, 32], F32, e)
    q_hi, e = place("q_hi", [P, 2, TILES * P], F32R, r1)
    q_lo, e = place("q_lo", [P, 2, TILES * P], F32R, e)
    k_hi, e = place("k_hi", [P, 2, NKEY + P], F32R, e)
    k_lo, e = place("k_lo", [P, 2, NKEY + P], F32R, e)
    v_hl, e = place("v_hl", [P, 2, 7, 2 * DH], F32R, e)
    pt0 = e
    pt_hi, e = place("pt_hi", [P, 2, NKEY], F32R, e)
    pt_lo, e = place("pt_lo", [P, 2, NKEY], F32R, e)
    assert e <= r1 + 4 * 12800
    gate_raw2, _ = place("gate_raw2", [P, 3, D_MODEL // 2], F32, pt0)
    y_sb, e = place("y_sb", [P, TILES, D_MODEL], F32, r1)
    gf_b, e = place("gf_b", [P, D_MODEL], F32, e)
    r2 = region(4 * TILES * D_MODEL)
    x_sb, e = place("x_sb", [P, TILES, D_MODEL], F32, r2)
    zs, e = place("zs", [P, TILES, NCOL], F32, r2)
    x_add, _ = place("x_add", [P, TILES, NCOL], F32, r2)
    kv_raw, e = place("kv_raw", [P, 2, 2, 2 * DH], F32, e)
    s0 = e
    s_sb, e = place("s_sb", [P, 2, 2, NKEY], F32, e)
    rope_t, _ = place("rope_t", [P, 4, LAT * NCOL // 4], F32, s0)
    sq_t, _ = place("sq_t", [P, TILES, 2 * DH], F32, s0)
    gate_raw1, _ = place("gate_raw1", [P, 3, D_MODEL // 2], F32, s0)
    sg, e = place("sg", [P, TILES, 2 * DH], F32, e)
    og, e = place("og", [P, TILES, 2 * DH], F32, e)
    o_sum, e = place("o_sum", [P, 2, 2 * DH], F32, e)
    sq_o, e = place("sq_o", [P, 2, DH], F32, e)
    assert e <= r2 + 4 * TILES * D_MODEL
    y_junk, _ = place("y_junk", [P, NCOL], F32, s0)
    rs0 = region(4 * 2 * TILES * P)
    row_st, _ = place("row_st", [P, 2, TILES * P], F32, rs0)
    gate_b, _ = place("gate_b", [P, 2, NCOL], F32, rs0)
    rope_a = new("rope_a", [P, 2, LAT, DK_A // 2])
    rope_b = new("rope_b", [P, 2, LAT, DH // 2])
    ident = new("ident", [P, P])
    norms = new("norms", [P, 3, DH])
    ada_rows = new("ada_rows", [P, 512])
    vec = new("vec", [P, 96])
    cs = new("cs", [P, 32])
    mod_a = new("mod_a", [P, 2, KT])
    mod_b = new("mod_b", [P, 2, KT])
    lam = new("lam", [P, 4, H_A])
    small = new("small", [P, 6, 4, 2])
    stat = new("stat", [P, 2, 16])
    half = new("half", [P, 16])
    ssq = new("ssq", [P, TILES, 4])
    nmax, den, rden, fac, ms, rstd = (small[:, i] for i in range(6))

    with ExitStack() as ctx:
        z_ps = ctx.enter_context(nc.psum_tensor("z_ps", [P, TILES, NCOL], F32))
        ring = [ctx.enter_context(nc.psum_tensor(f"ring{b}", [P, 512], F32)) for b in range(RING)]

        def sem(name):
            return ctx.enter_context(nc.semaphore(name))

        x_in = [sem(f"x_in{t}") for t in range(TILES)]
        vec_in, lam_in, rope_in, norm_in = sem("vec_in"), sem("lam_in"), sem("rope_in"), sem("norm_in")
        ada_in = [sem(f"ada_in{b}") for b in range(ADA_RING)]
        raw_in = [sem(f"raw_in{b}") for b in range(RAW_RING)]
        ada_used = sem("ada_used")
        id_set = sem("id_set")
        cs_step, cs_ready, mod_ready = sem("cs_step"), sem("cs_ready"), sem("mod_ready")
        x_sq, x_rstd, x_hat = sem("x_sq"), sem("x_rstd"), sem("x_hat")
        h_mod, h_hi, h_lo = sem("h_mod"), sem("h_hi"), sem("h_lo")
        w_hi_done, w_lo_done = sem("w_hi_done"), sem("w_lo_done")
        tile_done, z_full, z_free = sem("tile_done"), sem("z_full"), sem("z_free")
        bank_full = [sem(f"bank_full{b}") for b in range(RING)]
        bank_free = [sem(f"bank_free{b}") for b in range(RING)]
        act_chain, dve_chain, pool_chain = sem("act_chain"), sem("dve_chain"), sem("pool_chain")
        kv_in = sem("kv_in")
        qk_ready = sem("qk_ready")
        qk_hi_done = sem("qk_hi_done")
        v_hi_done, v_lo_done = sem("v_hi_done"), sem("v_lo_done")
        sq_ready, zr_ready, zn_ready = sem("sq_ready"), sem("zr_ready"), sem("zn_ready")
        g_exp, g_one, g_inv, g_ready = sem("g_exp"), sem("g_one"), sem("g_inv"), sem("g_ready")
        max_ready, exp_done, p_ready = sem("max_ready"), sem("exp_done"), sem("p_ready")
        pt_hi_done = sem("pt_hi_done")
        o_part, o_sq, o_rstd, og_ready = sem("o_part"), sem("o_sq"), sem("o_rstd"), sem("og_ready")
        row_out, row_in = ([sem(f"row_{w}{b}") for b in range(2)] for w in ("out", "in"))
        o_hi_done, o_lo_done = sem("o_hi_done"), sem("o_lo_done")
        state_out = sem("state_out")
        lam_ready = sem("lam_ready")
        gate_in = [sem(f"gate_in{b}") for b in range(6)]
        gate_used, gate_bias, gate_out = sem("gate_used"), sem("gate_bias"), sem("gate_out")
        gate_b_in, x_add_in, gf_in = sem("gate_b_in"), sem("x_add_in"), sem("gf_in")
        y_mul, y_add, y_sq, y_rstd, y_ready, y_out = (
            sem("y_mul"), sem("y_add"), sem("y_sq"), sem("y_rstd"), sem("y_ready"), sem("y_out"))

        def wait_full(eng, n):
            eng.wait_ge(bank_full[n % RING], n // RING + 1)

        def wait_free(eng, n):
            eng.wait_ge(bank_free[n % RING], n // RING + 1)

        def wait_tile(eng, kg):
            it, s = divmod(kg, KT)
            if s == KT - 1:
                eng.wait_ge(z_full, TILES * (it + 1))
            else:
                eng.wait_ge(tile_done, (KT - 1) * it + s + 1)

        def linker(eng, s):
            n = [0]

            def link(ins):
                n[0] += 1
                ins.then_inc(s, 1)
                eng.wait_ge(s, n[0])
            return link

        def heads(a):
            return 2 if group_kind(a) == "G" else 1

        def n_step(a, t):
            return TILES * (a if a < KV_IT else a - 1) + t

        def attn_groups_before(a):
            return a if a < KV_IT else a - 1

        N_VH = [1 if group_kind(a) == "D" else 2 if group_kind(a) == "KV" else 0 for a in range(OUT_IT)]

        def qk_parts(a):
            n = TURN[("QK", a, 0)]
            g = group_kind(a)
            S, C = LAT * P, PAST * P
            if g == "D":
                return [(n, 0, S, q_hi[:, 0, 0:S], q_lo[:, 0, 0:S], True),
                        (n + 1, 0, S, k_hi[:, 0, 0:S], k_lo[:, 0, 0:S], True),
                        (n + 2, 0, C + P, k_hi[:, 0, S:S + C + P], k_lo[:, 0, S:S + C + P], False),
                        (n + 2, C + P, P, q_hi[:, 0, S:S + P], q_lo[:, 0, S:S + P], True)]
            if g == "KV":
                return [(n + c, 0, S, k_hi[:, c, 0:S], k_lo[:, c, 0:S], True) for c in range(2)] + \
                    [(n + 2 + c, 0, C + P, k_hi[:, c, S:S + C + P], k_lo[:, c, S:S + C + P], True) for c in range(2)]
            return [(n + c, 0, S, q_hi[:, c, 0:S], q_lo[:, c, 0:S], True) for c in range(2)] + \
                [(n + 2, P * c, P, q_hi[:, c, S:S + P], q_lo[:, c, S:S + P], c == 1) for c in range(2)]

        QKP = [len(qk_parts(a)) for a in range(OUT_IT)]

        def t_parts(a, t):
            n = TURN[("T", a, t)]
            hs = range(heads(a))
            if t == 0:
                return [(n, c, 0, 1, P * c, c == heads(a) - 1) for c in hs]
            return [(n + 2 * c + j // 4, c, j, m, 0, True) for c in hs for j, m in ((0, 4), (4, 2))]

        PT_BEFORE = {}
        npt = 0
        for it_ in range(ITS):
            for s_ in range(KT):
                for kind_, a_, t_ in steps_at(it_, s_):
                    if kind_ == "T":
                        PT_BEFORE[(a_, t_)] = npt
                        npt += len(t_parts(a_, t_))

        V_DONE, OG_DONE, G_DONE, ROW_DONE = [], [], [], []
        v = o_ = gg = ro = 0
        for a in range(OUT_IT):
            v += 2 * N_VH[a]
            V_DONE.append(v)
            if group_kind(a) != "KV":
                o_ += TILES * heads(a)
                gg += TILES
            OG_DONE.append(o_)
            G_DONE.append(gg)
            ro += heads(a) if group_kind(a) != "KV" else 0
            ROW_DONE.append(ro)

        STATE_DONE = [32 * min(a + 1, G_IT) for a in range(OUT_IT)]

        def before(table, a):
            return table[a - 1] if a else 0

        def og_index(a, t, c_):
            return before(OG_DONE, a) + heads(a) * t + c_

        N_SPILL = ROW_DONE[G_IT + 1]
        assert N_SPILL == 12

        block = ctx.enter_context(nc.Block())

        @block.sync
        def _(sp):
            sp.dma_start(vec_rows[0:16, :], c[0].rearrange("(k q) -> k q", q=P)).then_inc(vec_in, 16)
            sp.dma_start(vec_rows[16:32, :], c_ctx.rearrange("(k q) -> k q", q=P)).then_inc(vec_in, 16)
            sp.dma_start(vec_rows[32:48, :], g_norm[0].rearrange("(k q) -> k q", q=P)).then_inc(vec_in, 16)
            sp.dma_start(vec_rows[48:96, :], b_ada[0].rearrange("(k q) -> k q", q=P)).then_inc(vec_in, 16)

            def load_ada(n):
                third, k = (1, n) if n < KT else (0, n - KT)
                m = n - ADA_RING
                if m == KT - 1:
                    wait_full(sp, TURN["SCALE"])
                elif m >= 0:
                    sp.wait_ge(ada_used, m + 1 if m < KT else m)
                sp.dma_start(ada_raw[:, n % ADA_RING, :],
                             ada_v[k, :, third * D_MODEL:(third + 1) * D_MODEL]).then_inc(ada_in[n % ADA_RING], 16)

            def load_w(j):
                it, s = divmod(2 * j, KT)
                if j >= RAW_RING:
                    sp.wait_ge(w_lo_done, 2 * (j - RAW_RING) + 2)
                dst = w_raw[:, j % RAW_RING]
                if it < H_A:
                    for u in range(2):
                        sp.dma_start(dst[:, u, :].rearrange("p (s c) -> p s c", s=4),
                                     wa_v[it, :, s + u]).then_inc(raw_in[j % RAW_RING], 16)
                    return
                if it == KV_IT:
                    for u in range(2):
                        sp.dma_start(dst[:, u, :], w_v[:, s + u, KB0:KB0 + NCOL]).then_inc(raw_in[j % RAW_RING], 16)
                elif it < OUT_IT:
                    for u, c0 in enumerate((QB0, GB0)):
                        c0 += 2 * DH * (it - G_IT)
                        sp.dma_start(dst[:, :, 2 * DH * u:2 * DH * (u + 1)],
                                     w_v[:, s:s + 2, c0:c0 + 2 * DH]).then_inc(raw_in[j % RAW_RING], 16)
                else:
                    c0 = NCOL * (it - OUT_IT)
                    for u in range(2):
                        sp.dma_start(dst[:, u, :], wo_v[:, s + u, c0:c0 + NCOL]).then_inc(raw_in[j % RAW_RING], 16)

            for n in range(ADA_RING):
                load_ada(n)
            for t in range(TILES):
                src = x_prompt[0] if t == 0 else xs_v[:, t - 1, :]
                sp.dma_start(x_sb[:, t, :], src).then_inc(x_in[t], 16)
                load_ada(ADA_RING + t)
            for n in range(ADA_RING + TILES, 2 * KT):
                load_ada(n)
                if n == 2 * KT - 4:
                    load_w(0)
                    load_w(1)
            for j in range(RAW_RING, ITS * KT // 2):
                load_w(j)

        @block.tensor
        def _(pe):
            def claim(n):
                if n >= RING:
                    pe.wait_ge(bank_free[n % RING], n // RING)
                return ring[n % RING]

            def filled(ins, n):
                ins.then_inc(bank_full[n % RING], 1)

            def split_matmul(out, hi_l, lo_l, hi_r, lo_r, start=True, stop=True):
                pe.matmul(out, hi_l, hi_r, start=start, stop=False)
                pe.matmul(out, hi_l, lo_r, start=False, stop=False)
                return pe.matmul(out, lo_l, hi_r, start=False, stop=stop)

            pe.wait_ge(id_set, 2)
            pe.wait_ge(vec_in, 64)
            n = TURN["VEC"]
            filled(pe.transpose(claim(n)[:, 0:96], vec_rows[:, :], ident[0:96, 0:96]), n)
            pe.wait_ge(cs_ready, 1)
            csv = cs[:, :].rearrange("p (r k) -> p k r", r=2)
            for third, key in enumerate(("SCALE", "SHIFT")):
                n = TURN[key]
                bank = claim(n)
                for k in range(KT):
                    m = third * KT + k
                    pe.wait_ge(ada_in[m % ADA_RING], 16 * (m // ADA_RING + 1))
                    for j in range(4):
                        ins = pe.matmul(bank[32 * j:32 * j + 2, :], csv[:, k, :],
                                        ada_raw[:, m % ADA_RING, 512 * j:512 * (j + 1)],
                                        start=(k == 0), stop=(k == KT - 1))
                    if k == KT - 1:
                        filled(ins, n)
                    else:
                        ins.then_inc(ada_used, 1)
            for third in range(2):
                n = TURN["COLS"] + third
                wait_free(pe, TURN["SHIFT" if third else "SCALE"])
                bank = claim(n)
                for b in range(4):
                    ins = pe.transpose(bank[:, P * b:P * (b + 1)], ada_rows[:, P * b:P * (b + 1)], ident[:, :])
                filled(ins, n)

            def h_transposes(kt):
                if kt == 0:
                    pe.wait_ge(x_hat, TILES)
                n = TURN[("HT", kt)]
                bank = claim(n)
                for t in range(1, TILES):
                    ins = pe.transpose(bank[:, P * (t - 1):P * t], x_sb[:, t, P * kt:P * (kt + 1)], ident[:, :])
                filled(ins, n)
                filled(pe.transpose(claim(n + 1)[:, 0:P], x_sb[:, 0, P * kt:P * (kt + 1)], ident[:, :]), n + 1)

            def project(it, s):
                kg = it * KT + s
                pe.wait_ge(w_lo_done, kg + 1)
                if it == 0:
                    pe.wait_ge(h_lo, s + 1)
                if it == OUT_IT and s < N_SPILL:
                    pe.wait_ge(o_lo_done, s + 1)
                elif it == OUT_IT:
                    a, c_ = OUT_IT - 2 + (s - N_SPILL) // 2, (s - N_SPILL) % 2
                    for u in range(2):
                        wait_free(pe, TURN[("O", a, 0)] + 2 * c_ + u)
                b = kg % W_RING
                for t in range(TILES):
                    if s == 0 and it:
                        pe.wait_ge(z_free, TILES * (it - 1) + t + 1)
                    tok = slice(P * t, P * (t + 1))
                    ins = split_matmul(z_ps[:, t, :], xt_hi[:, s, tok], xt_lo[:, s, tok], w_hi[:, b, :],
                                       w_lo[:, b, :], start=(s == 0), stop=(s == KT - 1))
                    if s == KT - 1:
                        ins.then_inc(z_full, 1)
                if s < KT - 1:
                    ins.then_inc(tile_done, 1)

            def step_qk(a):
                n = TURN[("QK", a, 0)]
                g = group_kind(a)
                pe.wait_ge(qk_ready, a + 1)
                if g != "G":
                    pe.wait_ge(kv_in, 32 * (a + 1))

                def tr(bank, col, src):
                    return pe.transpose(bank[:, col:col + P], src, ident[:, :])
                if g == "D":
                    for u in range(2):
                        bank = claim(n + u)
                        for t in range(1, TILES):
                            ins = tr(bank, P * (t - 1), zs[:, t, DH * u:DH * (u + 1)])
                        filled(ins, n + u)
                    bank = claim(n + 2)
                    for j in range(PAST):
                        tr(bank, P * j, kv_raw[:, 0, j, 0:DH])
                    tr(bank, P * PAST, zs[:, 0, DH:2 * DH])
                    filled(tr(bank, P * PAST + P, zs[:, 0, 0:DH]), n + 2)
                    return
                for c_ in range(2):
                    bank = claim(n + c_)
                    for t in range(1, TILES):
                        ins = tr(bank, P * (t - 1), zs[:, t, DH * c_:DH * (c_ + 1)])
                    filled(ins, n + c_)
                if g == "KV":
                    for c_ in range(2):
                        bank = claim(n + 2 + c_)
                        for j in range(PAST):
                            tr(bank, P * j, kv_raw[:, 0, j, DH * c_:DH * (c_ + 1)])
                        filled(tr(bank, P * PAST, zs[:, 0, DH * c_:DH * (c_ + 1)]), n + 2 + c_)
                    return
                bank = claim(n + 2)
                for c_ in range(2):
                    ins = tr(bank, P * c_, zs[:, 0, DH * c_:DH * (c_ + 1)])
                filled(ins, n + 2)

            def step_s(a, t):
                n = TURN[("S", a, t)]
                if t == 0:
                    for u in range(3):
                        wait_free(pe, TURN[("QK", a, 0)] + u)
                q0 = LAT * P if t == 0 else P * (t - 1)
                parts = [(NKEY, P)] if t == 0 else [(0, 512), (512, 256)]
                for c_ in range(2):
                    for k0, kn in parts:
                        bank = claim(n)
                        if group_kind(a) == "D":
                            rows, qh, kh = slice(DK_A * c_, DK_A * (c_ + 1)), 0, 0
                        else:
                            rows, qh, kh = slice(0, P), c_, (a - G_IT) // 2
                        ins = split_matmul(bank[:, 0:kn], q_hi[rows, qh, q0:q0 + P], q_lo[rows, qh, q0:q0 + P],
                                           k_hi[rows, kh, k0:k0 + kn], k_lo[rows, kh, k0:k0 + kn])
                        filled(ins, n)
                        n += 1

            def step_t(a, t):
                pe.wait_ge(p_ready, n_step(a, t) + 1)
                for n, c_, j0, m, col, last in t_parts(a, t):
                    bank = claim(n) if col == 0 else ring[n % RING]
                    for j in range(m):
                        ins = pe.transpose(bank[:, col + P * j:col + P * (j + 1)],
                                           s_sb[:, n_step(a, t) % 2, c_, P * (j0 + j):P * (j0 + j + 1)], ident[:, :])
                    if last:
                        filled(ins, n)

            def step_v(a, t):
                n = TURN[("V", a, t)]
                pe.wait_ge(v_lo_done, V_DONE[a])
                for m, *_ in t_parts(a, t):
                    wait_free(pe, m)
                bank = claim(n)
                tiles = [(0, 0)] if t == 0 else [(j, j + 1) for j in range(LAT + PAST)]
                vh = 0 if group_kind(a) == "D" else (a - G_IT) // 2
                for c_ in range(heads(a)):
                    o = 2 * DH * c_
                    for j, vt in tiles:
                        keys = slice(P * j, P * (j + 1))
                        pe.matmul(bank[:, o:o + 2 * DH], pt_hi[:, c_, keys], v_hl[:, vh, vt, :],
                                  start=(j == 0), stop=False, skip_group_check=True)
                        ins = pe.matmul(bank[:, o:o + DH], pt_lo[:, c_, keys], v_hl[:, vh, vt, 0:DH],
                                        start=False, stop=(j == tiles[-1][0]), skip_group_check=True)
                filled(ins, n)

            def step_o(a):
                n = TURN[("O", a, 0)]
                pe.wait_ge(og_ready, OG_DONE[a])
                for c_ in range(heads(a)):
                    bank = claim(n)
                    for t in range(1, TILES):
                        ins = pe.transpose(bank[:, P * (t - 1):P * t], og[:, t, DH * c_:DH * (c_ + 1)], ident[:, :])
                    filled(ins, n)
                    filled(pe.transpose(claim(n + 1)[:, 0:P], og[:, 0, DH * c_:DH * (c_ + 1)], ident[:, :]), n + 1)
                    n += 2

            def step_gate(s):
                n = TURN["GATE"]
                bank = claim(n) if s == GATE_SLOT else ring[n % RING]
                for m in gate_pieces(s):
                    k, u = divmod(m, 2)
                    pe.wait_ge(gate_in[m % 6], 16 * (m // 6 + 1))
                    buf = (gate_raw1 if m % 6 < 3 else gate_raw2)[:, m % 3, :]
                    for jj in range(2):
                        j = 2 * u + jj
                        ins = pe.matmul(bank[32 * j:32 * j + 2, :], csv[:, k, :], buf[:, 512 * jj:512 * (jj + 1)],
                                        start=(k == 0), stop=(k == KT - 1))
                    if m < 2 * KT - 1:
                        ins.then_inc(gate_used, 1)
                    else:
                        filled(ins, n)

            for kt in range(H_AHEAD):
                h_transposes(kt)
            for it in range(ITS):
                for s in range(KT):
                    if it == 0 and s + H_AHEAD < KT:
                        h_transposes(s + H_AHEAD)
                    project(it, s)
                    for kind, a, t in steps_at(it, s):
                        if kind == "QK":
                            step_qk(a)
                        elif kind == "S":
                            step_s(a, t)
                        elif kind == "T":
                            step_t(a, t)
                        elif kind == "V":
                            step_v(a, t)
                        else:
                            step_o(a)
                    if it == G_IT and s >= GATE_SLOT:
                        step_gate(s)

        def squares_y(act, m):
            cc, t = divmod(m, TILES)
            act.wait_ge(y_add, m + 1)
            if m:
                act.wait_ge(y_sq, m)
            act.activation(y_junk[:, :], y_sb[:, t, NCOL * cc:NCOL * (cc + 1)], ACT.Square,
                           accum_out=ssq[:, t, cc:cc + 1]).then_inc(y_sq, 1)

        @block.scalar
        def _(act):
            link = linker(act, act_chain)

            def copy(out, in_, **kw):
                return act.activation(out, in_, ACT.Copy, **kw)

            wait_free(act, TURN["VEC"])
            act.activation(cs_t[:, :], vec[:, 0:32], ACT.Exp, scale=-1.0).then_inc(cs_step, 1)
            for t in range(TILES):
                act.wait_ge(x_in[t], 16)
                if t:
                    act.wait_ge(x_sq, t)
                act.activation(z_ps[:, 0:4, :], x_sb[:, t, :].rearrange("p (b n) -> p b n", b=4), ACT.Square,
                               accum_out=stat[:, 0, t:t + 1]).then_inc(x_sq, 1)
            act.wait_ge(lam_ready, 1)
            act.activation(lam[:, 2:4, :], lam[:, 0:2, :], ACT.Exp).then_inc(lam_ready, 1)

            def modulate(kt):
                if kt == 0:
                    act.wait_ge(mod_ready, 2)
                    wait_free(act, TURN["COLS"] + 1)
                n = TURN[("HT", kt)]
                if kt >= 2:
                    act.wait_ge(h_lo, kt - 1)
                wait_full(act, n)
                act.activation(row_st[:, kt % 2, P:], ring[n % RING][:, 0:LAT * P], ACT.Identity,
                               bias=mod_b[:, 0, kt:kt + 1], scale=mod_a[:, 0, kt:kt + 1]).then_inc(bank_free[n % RING], 1)
                n += 1
                wait_full(act, n)
                act.activation(row_st[:, kt % 2, 0:P], ring[n % RING][:, 0:P], ACT.Identity,
                               bias=mod_b[:, 1, kt:kt + 1], scale=mod_a[:, 1, kt:kt + 1]).then_inc(bank_free[n % RING], 1)

            def split_w(kg):
                j = kg // 2
                act.wait_ge(raw_in[j % RAW_RING], 32 * (j // RAW_RING + 1))
                if kg >= W_RING:
                    wait_tile(act, kg - W_RING)
                copy(w_hi[:, kg % W_RING, :], w_raw[:, j % RAW_RING, kg % 2, :]).then_inc(w_hi_done, 1)

            def z_out(it):
                if it:
                    act.wait_ge(qk_ready, it)
                    act.wait_ge(v_lo_done, V_DONE[it - 1])
                    act.wait_ge(g_ready, G_DONE[it - 1])
                    act.wait_ge(state_out, STATE_DONE[it - 1])
                    n = TURN[("QK", it - 1, 0)] + banks_of("QK", it - 1, 0) - 1
                    wait_free(act, n)
                for t in range(TILES):
                    act.wait_ge(z_full, TILES * it + t + 1)
                    copy(zs[:, t, :], z_ps[:, t, :]).then_inc(z_free, 1)

            def v_hi(a):
                g = group_kind(a)
                if g == "G":
                    return
                act.wait_ge(z_free, TILES * (a + 1))
                for c_ in range(N_VH[a]):
                    v0 = (2 * DH if g == "D" else 2 * DH + DH * c_)
                    copy(v_hl[:, c_, 0:TILES, 0:DH], zs[:, :, v0:v0 + DH]).then_inc(v_hi_done, 1)
                act.wait_ge(kv_in, 32 * (a + 1))
                for c_ in range(N_VH[a]):
                    copy(v_hl[:, c_, TILES:, 0:DH], kv_raw[:, 1, :, DH * c_:DH * (c_ + 1)]).then_inc(v_hi_done, 1)

            def gate_exp(a):
                if group_kind(a) == "KV":
                    return
                act.wait_ge(z_free, TILES * (a + 1))
                act.wait_ge(og_ready, before(OG_DONE, a))
                w = DH * heads(a)
                act.activation(sg[:, :, 0:w], zs[:, :, NCOL - w:NCOL], ACT.Exp, scale=-1.0).then_inc(g_exp, 1)

            def qk_his(a):
                for n, col, w, hi, _, _ in qk_parts(a):
                    wait_full(act, n)
                    copy(hi, ring[n % RING][:, col:col + w]).then_inc(qk_hi_done, 1)

            def scores_out(a, t):
                n = TURN[("S", a, t)]
                scale = DK_A ** -0.5 if group_kind(a) == "D" else DH ** -0.5
                parts = [(0, P)] if t == 0 else [(0, 512), (512, 256)]
                for c_ in range(2):
                    for k0, kn in parts:
                        wait_full(act, n)
                        copy(s_sb[:, n_step(a, t) % 2, c_, k0:k0 + kn], ring[n % RING][:, 0:kn],
                             scale=scale).then_inc(bank_free[n % RING], 1)
                        n += 1

            def exps(a, t):
                m = n_step(a, t)
                act.wait_ge(max_ready, m + 1)
                kn = NKEY if t else P
                for c_ in range(2):
                    row = s_sb[:, m % 2, c_, 0:kn]
                    act.activation(row, row, ACT.Exp, bias=nmax[:, m % 4, c_:c_ + 1],
                                   accum_out=den[:, m % 4, c_:c_ + 1]).then_inc(exp_done, 1)

            def pt_his(a, t):
                for n, c_, j0, w, col, _ in t_parts(a, t):
                    wait_full(act, n)
                    copy(pt_hi[:, c_, P * j0:P * (j0 + w)], ring[n % RING][:, col:col + P * w]).then_inc(pt_hi_done, 1)

            def o_low(a, t):
                n = TURN[("V", a, t)]
                m = n_step(a, t)
                act.wait_ge(og_ready, og_index(a, t, 0) - heads(a) if t >= 2 else before(OG_DONE, a))
                wait_full(act, n)
                h = heads(a)
                copy(o_sum[:, m % 2, 0:DH * h].rearrange("p (c d) -> p c d", c=h),
                     ring[n % RING][:, 0:2 * DH * h].rearrange("p (c u d) -> p c u d", c=h, u=2)[:, :, 1, :]
                     ).then_inc(o_part, 1)

            def o_squares(a, t):
                if group_kind(a) != "D":
                    return
                m = n_step(a, t)
                wait_free(act, TURN[("V", a, t)])
                act.activation(sq_o[:, m % 2, :], o_sum[:, m % 2, 0:DH], ACT.Square, scale=rden[:, m % 4, 0:1],
                               accum_out=ms[:, m % 4, 0:1]).then_inc(o_sq, 1)

            def rows_out(a):
                n = TURN[("O", a, 0)]
                for c_ in range(heads(a)):
                    r = before(ROW_DONE, a) + c_
                    if r < N_SPILL:
                        if r >= 2:
                            act.wait_ge(row_out[r % 2], 16 * (r // 2))
                        else:
                            act.wait_ge(h_lo, KT)
                        wait_full(act, n)
                        copy(row_st[:, r % 2, P:], ring[n % RING][:, 0:LAT * P]).then_inc(bank_free[n % RING], 1)
                        wait_full(act, n + 1)
                        copy(row_st[:, r % 2, 0:P], ring[(n + 1) % RING][:, 0:P]).then_inc(bank_free[(n + 1) % RING], 1)
                    else:
                        wait_tile(act, KT * OUT_IT - 1)
                        wait_full(act, n)
                        copy(xt_hi[:, r, P:], ring[n % RING][:, 0:LAT * P]).then_inc(o_hi_done, 1)
                        wait_full(act, n + 1)
                        copy(xt_hi[:, r, 0:P], ring[(n + 1) % RING][:, 0:P]).then_inc(o_hi_done, 1)
                    n += 2

            def row_hi(r):
                act.wait_ge(row_in[r % 2], 16 * (r // 2 + 1))
                wait_tile(act, KT * (OUT_IT - 1) + r)
                copy(xt_hi[:, r, :], row_st[:, r % 2, :]).then_inc(o_hi_done, 1)

            for kg in range(W_AHEAD):
                split_w(kg)
            for kt in range(H_AHEAD):
                modulate(kt)
            late = []
            for it in range(ITS):
                for s in range(KT):
                    if it == 0 and s + H_AHEAD < KT:
                        modulate(s + H_AHEAD)
                    for kind, a, t in late:
                        if kind == "S":
                            exps(a, t)
                        if kind == "V":
                            o_squares(a, t)
                    late = steps_at(it, s)
                    kg = it * KT + s + W_AHEAD
                    if s == 0 and 0 < it <= OUT_IT:
                        z_out(it - 1)
                    if kg < ITS * KT:
                        split_w(kg)
                    if s == 1 and 0 < it <= OUT_IT:
                        v_hi(it - 1)
                        gate_exp(it - 1)
                    for kind, a, t in late:
                        if kind == "QK":
                            qk_his(a)
                        elif kind == "S":
                            scores_out(a, t)
                        elif kind == "T":
                            pt_his(a, t)
                        elif kind == "V":
                            o_low(a, t)
                        elif kind == "O":
                            rows_out(a)
                        if it == OUT_IT and s == 13 and kind == "V":
                            o_squares(a, t)
                    if it == OUT_IT and s == 13:
                        late = []
                    if it == OUT_IT - 1 and 3 <= s < 3 + N_SPILL:
                        row_hi(s - 3)
                    if it > OUT_IT and s < TILES:
                        m = TILES * (it - OUT_IT - 1) + s
                        squares_y(act, m)
            for t in range(TILES):
                squares_y(act, TILES * (OUTS - 1) + t)

        @block.vector
        def _(dve):
            link = linker(dve, dve_chain)
            link(dve.memset(ada_rows[:, :], 0.0))
            n = TURN["VEC"]
            wait_full(dve, n)
            dve.tensor_copy(vec[:, :], ring[n % RING][:, 0:96]).then_inc(bank_free[n % RING], 1)
            wait_free(dve, n)
            dve.wait_ge(cs_step, 1)
            link(dve.tensor_scalar(cs[:, :], cs_t[:, :], 1.0, None, ALU.add))
            link(dve.reciprocal(cs_t[:, :], cs[:, :]))
            dve.tensor_tensor(cs[:, :], vec[:, 0:32], cs_t[:, :], ALU.mult).then_inc(cs_ready, 1)
            dve.wait_ge(lam_in, 64)
            link(dve.tensor_tensor(lam_raw[:, 0:2, :], lam_raw[:, 0:2, :], lam_raw[:, 2:4, :], ALU.mult))
            dve.tensor_reduce(lam[:, 0:2, :], lam_raw[:, 0:2, :].rearrange("p u (h d) -> p u h d", h=H_A), AX_X,
                              ALU.add).then_inc(lam_ready, 1)
            dve.wait_ge(lam_ready, 2)
            link(dve.tensor_tensor(lam[:, 0, :], lam[:, 3, :], lam[:, 2, :], ALU.subtract))
            link(dve.tensor_scalar(lam[:, 1, :], lam[:, 0, :], -LAM_INIT, None, ALU.add))
            dve.wait_ge(norm_in, 48)
            link(dve.tensor_scalar(norms[:, 0, :], norms[:, 0, :], 1.0 - LAM_INIT, None, ALU.mult))
            for t in range(TILES):
                dve.wait_ge(x_rstd, t + 1)
                dve.tensor_scalar(x_sb[:, t, :], x_sb[:, t, :], stat[:, 1, t:t + 1], None, ALU.mult).then_inc(x_hat, 1)
            for third, key in enumerate(("SCALE", "SHIFT")):
                n = TURN[key]
                wait_full(dve, n)
                if third:
                    wait_full(dve, TURN["COLS"])
                for j in range(4):
                    rows = slice(32 * j, 32 * j + 2)
                    ins = dve.tensor_copy(ada_rows[rows, :], ring[n % RING][rows, :])
                    if j < 3:
                        link(ins)
                ins.then_inc(bank_free[n % RING], 1)
                n = TURN["COLS"] + third
                wait_full(dve, n)
                cols = ring[n % RING][:, :].rearrange("p (b j q) -> p b j q", b=4, j=4)
                b0 = 48 + KT * (1 - third)
                bias = vec[:, b0:b0 + KT].rearrange("p (j b) -> p b j", b=4)
                for r in range(2):
                    dst = (mod_b if third else mod_a)[:, r, :].rearrange("p (j b) -> p b j", b=4)
                    for b in range(4):
                        ins = dve.scalar_tensor_tensor(dst[:, b, :], cols[:, b, :, r], 1.0 - third, bias[:, b, :],
                                                       ALU.add, ALU.add)
                        if r == 1 and b == 3:
                            ins.then_inc(bank_free[n % RING], 1)
                if third == 0:
                    wait_free(dve, n)
                    for r in range(2):
                        dst = mod_a[:, r, :]
                        dve.tensor_tensor(dst, dst, vec[:, 32:48], ALU.mult).then_inc(mod_ready, 1)

            def split_h(kt):
                n = TURN[("HT", kt)]
                wait_free(dve, n)
                wait_free(dve, n + 1)
                dve.tensor_copy(xt_hi[:, kt, :], row_st[:, kt % 2, :]).then_inc(h_hi, 1)
                dve.wait_ge(h_hi, kt + 1)
                dve.tensor_tensor(xt_lo[:, kt, :], row_st[:, kt % 2, :], xt_hi[:, kt, :].bitcast(F32),
                                  ALU.subtract).then_inc(h_lo, 1)

            def split_w(kg):
                dve.wait_ge(w_hi_done, kg + 1)
                b = kg % W_RING
                dve.tensor_tensor(w_lo[:, b, :], w_raw[:, kg // 2 % RAW_RING, kg % 2, :], w_hi[:, b, :].bitcast(F32),
                                  ALU.subtract).then_inc(w_lo_done, 1)

            def rotate(a):
                g = group_kind(a)
                dve.wait_ge(z_free, TILES * (a + 1))
                if a == G_IT:
                    wait_full(dve, TURN["GATE"])
                if g != "D":
                    z2 = zs[:, :, 0:2 * DH].rearrange("p t (c d) -> p t c d", c=2)
                    link(dve.tensor_tensor(sq_t[:, :, :], zs[:, :, 0:2 * DH], zs[:, :, 0:2 * DH], ALU.mult))
                    m = a - KV_IT
                    ss = stat[:, 0, 0:10].rearrange("p (t c) -> p t c", c=2)
                    dve.tensor_reduce(ss, sq_t[:, :, :].rearrange("p t (c d) -> p t c d", c=2), AX_X,
                                      ALU.add).then_inc(sq_ready, 1)
                    dve.wait_ge(zr_ready, m + 1)
                    rs = stat[:, 1, 0:10].rearrange("p (t c) -> p t c", c=2)
                    link(dve.tensor_tensor(z2, z2, rs.unsqueeze(3).broadcast_to([P, TILES, 2, DH]), ALU.mult))
                    w = norms[:, 2 if g == "KV" else 1, :]
                    dve.tensor_tensor(z2, z2, w.unsqueeze(1).unsqueeze(1).broadcast_to([P, TILES, 2, DH]),
                                      ALU.mult).then_inc(zn_ready, 1)
                    dve.wait_ge(zn_ready, m + 1)
                ng, half_d, tab = (4, DK_A // 2, rope_a) if g == "D" else (2, DH // 2, rope_b)
                zz = zs[:, 1:, 0:2 * DH].rearrange("p t (g u d) -> p t g u d", g=ng, u=2)
                x1, x2 = zz[:, :, :, 0, :], zz[:, :, :, 1, :]
                cos, sin = (tab[:, u].unsqueeze(2).broadcast_to([P, LAT, ng, half_d]) for u in range(2))
                tmp = [rope_t[:, u, :].rearrange("p (t g d) -> p t g d", t=LAT, g=ng) for u in range(4)]
                dve.wait_ge(rope_in, 32)
                dve.tensor_tensor(tmp[0], x1, cos, ALU.mult)
                dve.tensor_tensor(tmp[1], x2, sin, ALU.mult)
                dve.tensor_tensor(tmp[2], x1, sin, ALU.mult)
                link(dve.tensor_tensor(tmp[3], x2, cos, ALU.mult))
                link(dve.tensor_tensor(x1, tmp[0], tmp[1], ALU.subtract))
                dve.tensor_tensor(x2, tmp[2], tmp[3], ALU.add).then_inc(qk_ready, 1)

            def v_lo(a):
                g = group_kind(a)
                if g == "G":
                    return
                done = V_DONE[a] - 2 * N_VH[a]
                for c_ in range(N_VH[a]):
                    v0 = (2 * DH if g == "D" else 2 * DH + DH * c_)
                    dve.wait_ge(v_hi_done, done + c_ + 1)
                    dve.tensor_tensor(v_hl[:, c_, 0:TILES, DH:], zs[:, :, v0:v0 + DH],
                                      v_hl[:, c_, 0:TILES, 0:DH].bitcast(F32), ALU.subtract).then_inc(v_lo_done, 1)
                for c_ in range(N_VH[a]):
                    dve.wait_ge(v_hi_done, done + N_VH[a] + c_ + 1)
                    dve.tensor_tensor(v_hl[:, c_, TILES:, DH:], kv_raw[:, 1, :, DH * c_:DH * (c_ + 1)],
                                      v_hl[:, c_, TILES:, 0:DH].bitcast(F32), ALU.subtract).then_inc(v_lo_done, 1)

            def gate_inverse(a, t):
                w = DH * heads(a)
                dve.wait_ge(g_one, attn_groups_before(a) + 1)
                dve.reciprocal(sg[:, t, 0:w], sg[:, t, 0:w]).then_inc(g_inv, 1)

            def qk_los(a):
                q0 = sum(QKP[:a])
                turns = [part[0] for part in qk_parts(a)]
                for n, col, w, hi, lo, last in qk_parts(a):
                    dve.wait_ge(qk_hi_done, q0 + max(i for i, m in enumerate(turns) if m == n) + 1)
                    ins = dve.tensor_tensor(lo, ring[n % RING][:, col:col + w], hi.bitcast(F32), ALU.subtract)
                    if last:
                        ins.then_inc(bank_free[n % RING], 1)

            def score_max(a, t):
                m = n_step(a, t)
                n = TURN[("S", a, t)]
                for u in range(banks_of("S", a, t)):
                    wait_free(dve, n + u)
                dve.tensor_reduce(nmax[:, m % 4, :], s_sb[:, m % 2, :, 0:(NKEY if t else P)], AX_X, ALU.max,
                                  negate=True).then_inc(max_ready, 1)

            def combine(a, t):
                m = n_step(a, t)
                b = m % 4
                dve.wait_ge(exp_done, 2 * m + 2)
                ins = dve.reciprocal(rden[:, b, :], den[:, b, :])
                if group_kind(a) == "G":
                    ins.then_inc(p_ready, 1)
                    return
                link(ins)
                link(dve.tensor_scalar(fac[:, b, 0:1], rden[:, b, 1:2], den[:, b, 0:1], lam[:, 1, a:a + 1], ALU.mult,
                                       ALU.mult))
                kn = NKEY if t else P
                e1, e2 = s_sb[:, m % 2, 0, 0:kn], s_sb[:, m % 2, 1, 0:kn]
                dve.scalar_tensor_tensor(e1, e2, fac[:, b, 0:1], e1, ALU.mult, ALU.add).then_inc(p_ready, 1)

            def pt_los(a, t):
                turns = [part[0] for part in t_parts(a, t)]
                for n, c_, j0, w, col, last in t_parts(a, t):
                    dve.wait_ge(pt_hi_done, PT_BEFORE[(a, t)] + max(i for i, m in enumerate(turns) if m == n) + 1)
                    keys = slice(P * j0, P * (j0 + w))
                    ins = dve.tensor_tensor(pt_lo[:, c_, keys], ring[n % RING][:, col:col + P * w],
                                            pt_hi[:, c_, keys].bitcast(F32), ALU.subtract)
                    if last:
                        ins.then_inc(bank_free[n % RING], 1)

            def o_high(a, t):
                n = TURN[("V", a, t)]
                m = n_step(a, t)
                h = heads(a)
                dve.wait_ge(o_part, m + 1)
                o = o_sum[:, m % 2, 0:DH * h].rearrange("p (c d) -> p c d", c=h)
                dve.tensor_tensor(o, ring[n % RING][:, 0:2 * DH * h].rearrange("p (c u d) -> p c u d", c=h, u=2)[:, :, 0, :],
                                  o, ALU.add).then_inc(bank_free[n % RING], 1)

            def gated(a, t):
                m = n_step(a, t)
                dve.wait_ge(g_ready, before(G_DONE, a) + t + 1)
                if t == 0 and a and group_kind(a - 1) != "KV":
                    wait_full(dve, TURN[("O", a - 1, 0)] + banks_of("O", a - 1, 0) - 1)
                if group_kind(a) == "D":
                    dve.wait_ge(o_rstd, m + 1)
                    scale = [rstd[:, m % 4, 1:2]]
                else:
                    wait_free(dve, TURN[("V", a, t)])
                    scale = [rden[:, m % 4, c_:c_ + 1] for c_ in range(2)]
                for c_ in range(heads(a)):
                    d = slice(DH * c_, DH * (c_ + 1))
                    dve.scalar_tensor_tensor(og[:, t, d], o_sum[:, m % 2, d], scale[c_], sg[:, t, d], ALU.mult,
                                             ALU.mult).then_inc(og_ready, 1)

            def rows_lo(a):
                n = TURN[("O", a, 0)]
                for c_ in range(heads(a)):
                    r = before(ROW_DONE, a) + c_
                    if r >= N_SPILL:
                        for u, tok in enumerate((slice(P, None), slice(0, P))):
                            dve.wait_ge(o_hi_done, N_SPILL + 2 * (r - N_SPILL) + u + 1)
                            w = LAT * P if u == 0 else P
                            ins = dve.tensor_tensor(xt_lo[:, r, tok], ring[(n + u) % RING][:, 0:w],
                                                    xt_hi[:, r, tok].bitcast(F32), ALU.subtract)
                            ins.then_inc(bank_free[(n + u) % RING], 1)
                    n += 2

            def row_lo(r):
                dve.wait_ge(o_hi_done, r + 1)
                dve.tensor_tensor(xt_lo[:, r, :], row_st[:, r % 2, :], xt_hi[:, r, :].bitcast(F32),
                                  ALU.subtract).then_inc(o_lo_done, 1)

            def gate_rows_out():
                n = TURN["GATE"]
                dve.wait_ge(gate_bias, 128)
                wait_full(dve, n)
                for j in range(4):
                    rows = slice(32 * j, 32 * j + 2)
                    ins = dve.tensor_tensor(ada_rows[rows, :], ring[n % RING][rows, :], ada_rows[rows, :], ALU.add)
                ins.then_inc(bank_free[n % RING], 1)

            def y_out_of_psum(cc):
                dve.wait_ge(gate_b_in, 32 * (cc + 1))
                dve.wait_ge(x_add_in, 32 * (cc + 1))
                for t in range(TILES):
                    m = TILES * cc + t
                    dve.wait_ge(z_full, TILES * (OUT_IT + cc) + t + 1)
                    cols = y_sb[:, t, NCOL * cc:NCOL * (cc + 1)]
                    dve.tensor_tensor(cols, z_ps[:, t, :], gate_b[:, 0 if t else 1, :], ALU.mult).then_inc(z_free, 1)
                for t in range(TILES):
                    m = TILES * cc + t
                    cols = y_sb[:, t, NCOL * cc:NCOL * (cc + 1)]
                    dve.wait_ge(z_free, TILES * (OUT_IT + cc) + t + 1)
                    dve.tensor_tensor(cols, cols, x_add[:, t, :], ALU.add).then_inc(y_add, 1)

            for kg in range(W_AHEAD):
                split_w(kg)
            for kt in range(H_AHEAD):
                split_h(kt)
            late = []
            for it in range(ITS):
                for s in range(KT):
                    if it == 0 and s + H_AHEAD < KT:
                        split_h(s + H_AHEAD)
                    kg = it * KT + s + W_AHEAD
                    if it > OUT_IT and s == 0:
                        y_out_of_psum(it - OUT_IT - 1)
                    if kg < ITS * KT:
                        split_w(kg)
                    for kind, a, t in late:
                        if kind == "S":
                            combine(a, t)
                    old, late = late, steps_at(it, s)
                    if 0 < it <= OUT_IT:
                        if s == 1:
                            rotate(it - 1)
                        if s == 2:
                            v_lo(it - 1)
                        if 4 <= s < 4 + TILES and group_kind(it - 1) != "KV":
                            gate_inverse(it - 1, s - 4)
                    for kind, a, t in late:
                        if kind == "QK":
                            qk_los(a)
                        elif kind == "S":
                            score_max(a, t)
                        elif kind == "T":
                            pt_los(a, t)
                        elif kind == "V":
                            o_high(a, t)
                            if it == OUT_IT and s == 13:
                                gated(a, t)
                        elif kind == "O":
                            rows_lo(a)
                    for kind, a, t in old:
                        if kind == "V":
                            gated(a, t)
                    if it == G_IT and s == KT - 1:
                        gate_rows_out()
                    if it == OUT_IT and s == 13:
                        late = []
                    if it == OUT_IT - 1 and 3 <= s < 3 + N_SPILL:
                        row_lo(s - 3)
            y_out_of_psum(OUTS - 1)
            dve.wait_ge(gf_in, 16)
            for t in range(TILES):
                dve.wait_ge(y_rstd, t + 1)
                dve.scalar_tensor_tensor(y_sb[:, t, :], y_sb[:, t, :], stat[:, 1, t:t + 1], gf_b[:, :], ALU.mult,
                                         ALU.mult).then_inc(y_ready, 1)

        @block.gpsimd
        def _(pool):
            link = linker(pool, pool_chain)
            link(pool.memset(half[:, :], -0.5))
            pool.memset(ident[:, :], 0.0).then_inc(id_set, 1)
            pool.wait_ge(id_set, 1)
            pool.affine_select(out=ident[:, :], in_=ident[:, :], compare_op=ALU.not_equal, fill=1.0, base=0,
                               pattern=[[-1, P]], channel_multiplier=1).then_inc(id_set, 1)
            for i, v_ in enumerate((lam_q1, lam_q2, lam_k1, lam_k2)):
                pool.dma_start(lam_raw[:, i, :], v_.rearrange("a h d -> a (h d)").broadcast_to([P, H_A * DK_A])
                               ).then_inc(lam_in, 16)
            for i, v_ in enumerate((subln_g, q_norm_g, k_norm_g)):
                pool.dma_start(norms[:, i, :], v_.broadcast_to([P, DH])).then_inc(norm_in, 16)
            pool.dma_start(rope_a[:, :, :, :], ropes_a).then_inc(rope_in, 16)
            pool.dma_start(rope_b[:, :, :, :], ropes_b).then_inc(rope_in, 16)

            def inv_root(out, in_, n, mean_of):
                link(pool.tensor_scalar(out, in_, 1.0 / mean_of, EPS, ALU.mult, ALU.add))
                return pool.tensor_tensor(out, out, half[:, 0:n], ALU.pow)

            for t in range(TILES):
                pool.wait_ge(x_sq, t + 1)
                inv_root(stat[:, 1, t:t + 1], stat[:, 0, t:t + 1], 1, D_MODEL).then_inc(x_rstd, 1)

            def load_kv(a):
                g = group_kind(a)
                if g == "G":
                    return
                if a:
                    pool.wait_ge(v_lo_done, V_DONE[a - 1])
                    n = TURN[("QK", a - 1, 0)]
                    for u in range(banks_of("QK", a - 1, 0)):
                        wait_free(pool, n + u)
                    pool.wait_ge(kv_in, 32 * a)
                else:
                    pool.wait_ge(x_hat, TILES)
                    n = TURN[("HT", KT - 1)]
                    wait_free(pool, n)
                    wait_free(pool, n + 1)
                for u, src in enumerate((dk_v, dv_v) if g == "D" else (gk_v, gv_v)):
                    if g == "D":
                        pool.dma_start(kv_raw[:, u, :, 0:DH], src[:, :, a, :]).then_inc(kv_in, 16)
                    else:
                        pool.dma_start(kv_raw[:, u].rearrange("p j (h d) -> p j h d", h=2), src).then_inc(kv_in, 16)

            def state(it):
                g = group_kind(it)
                if g == "D":
                    pool.wait_ge(z_free, TILES * it + 1)
                    pool.dma_start(new_dk[0, 0, :, it, :], zs[:, 0, DH:2 * DH]).then_inc(state_out, 16)
                    pool.dma_start(new_dv[0, 0, :, it, :], zs[:, 0, 2 * DH:3 * DH]).then_inc(state_out, 16)
                elif g == "KV":
                    pool.wait_ge(zn_ready, 1)
                    pool.dma_start(new_gk[0, 0].rearrange("s h d -> s (h d)"), zs[:, 0, 0:2 * DH]).then_inc(state_out, 16)
                    pool.dma_start(new_gv[0, 0].rearrange("s h d -> s (h d)"), zs[:, 0, 2 * DH:]).then_inc(state_out, 16)

            def gate_one(a):
                pool.wait_ge(g_exp, attn_groups_before(a) + 1)
                w = DH * heads(a)
                pool.tensor_scalar(sg[:, :, 0:w], sg[:, :, 0:w], 1.0, None, ALU.add).then_inc(g_one, 1)

            def gate_mul(a, t):
                w = DH * heads(a)
                pool.wait_ge(g_inv, before(G_DONE, a) + t + 1)
                ins = pool.tensor_tensor(sg[:, t, 0:w], sg[:, t, 0:w], zs[:, t, NCOL - w:NCOL], ALU.mult)
                if group_kind(a) == "D":
                    link(ins)
                    ins = pool.tensor_tensor(sg[:, t, 0:w], sg[:, t, 0:w], norms[:, 0, :], ALU.mult)
                ins.then_inc(g_ready, 1)

            def o_root(a, t):
                if group_kind(a) != "D":
                    return
                m = n_step(a, t)
                pool.wait_ge(o_sq, m + 1)
                link(inv_root(rstd[:, m % 4, 0:1], ms[:, m % 4, 0:1], 1, DH))
                pool.tensor_tensor(rstd[:, m % 4, 1:2], rstd[:, m % 4, 0:1], rden[:, m % 4, 0:1],
                                   ALU.mult).then_inc(o_rstd, 1)

            def spill(a):
                n = TURN[("O", a, 0)]
                for c_ in range(heads(a)):
                    r = before(ROW_DONE, a) + c_
                    if r < N_SPILL:
                        wait_free(pool, n)
                        wait_free(pool, n + 1)
                        pool.dma_start(o_spill[r], row_st[:, r % 2, :]).then_inc(row_out[r % 2], 16)
                    n += 2

            def load_row(r):
                if r < 2:
                    pool.wait_ge(row_out[r], 16 * N_SPILL // 2)
                else:
                    pool.wait_ge(o_lo_done, r - 1)
                pool.dma_start(row_st[:, r % 2, :], o_spill[r]).then_inc(row_in[r % 2], 16)

            def load_gate(m):
                k, u = divmod(m, 2)
                if m >= 6:
                    pool.wait_ge(gate_used, m - 5)
                dst = (gate_raw1 if m % 6 < 3 else gate_raw2)[:, m % 3, :]
                c0 = 2 * D_MODEL + u * (D_MODEL // 2)
                pool.dma_start(dst, ada_v[k, :, c0:c0 + D_MODEL // 2]).then_inc(gate_in[m % 6], 16)

            def load_out_operands(cc):
                if cc:
                    pool.wait_ge(y_add, TILES * cc)
                else:
                    pool.wait_ge(g_ready, G_DONE[OUT_IT - 1])
                    wait_free(pool, TURN[("QK", OUT_IT - 1, 0)] + 2)
                cols = slice(NCOL * cc, NCOL * (cc + 1))
                pool.dma_start(x_add[:, 0, :], x_prompt[0, :, cols]).then_inc(x_add_in, 16)
                pool.dma_start(x_add[:, 1:, :], xs_v[:, :, cols]).then_inc(x_add_in, 16)
                for r in range(2):
                    pool.dma_start(gate_b[:, r, :], gate_rows[r:r + 1, cols].broadcast_to([P, NCOL])
                                   ).then_inc(gate_b_in, 16)

            load_kv(0)
            late = []
            for it in range(ITS):
                for s in range(KT):
                    if 0 < it <= OUT_IT:
                        if s == 0 and group_kind(it - 1) == "D":
                            state(it - 1)
                        if s == 1 and it > KV_IT:
                            m = it - 1 - KV_IT
                            pool.wait_ge(sq_ready, m + 1)
                            inv_root(stat[:, 1, 0:10], stat[:, 0, 0:10], 10, DH).then_inc(zr_ready, 1)
                        if s == 2 and it - 1 == KV_IT:
                            state(it - 1)
                        if s == 1 and group_kind(it - 1) != "KV":
                            gate_one(it - 1)
                        if 4 <= s < 4 + TILES and group_kind(it - 1) != "KV":
                            gate_mul(it - 1, s - 4)
                        if s == 5 and it < OUT_IT:
                            load_kv(it)
                    if it == OUT_IT - 1 and s >= 2 and s - 2 < N_SPILL:
                        load_row(s - 2)
                    if it == G_IT and s == GATE_SLOT:
                        for j in range(4):
                            for r in range(2):
                                c0 = 2 * D_MODEL + 512 * j
                                pool.dma_start(ada_rows[32 * j + r:32 * j + r + 1, :], b_ada[:, c0:c0 + 512]
                                               ).then_inc(gate_bias, 16)
                        pool.wait_ge(qk_ready, G_IT)
                        wait_full(pool, TURN[("V", H_A - 1, TILES - 1)])
                        for m in range(2 * KT):
                            load_gate(m)
                        wait_free(pool, TURN["GATE"])
                        for j in range(4):
                            pool.dma_start(gate_rows[:, 512 * j:512 * (j + 1)], ada_rows[32 * j:32 * j + 2, :]
                                           ).then_inc(gate_out, 16)
                    for kind, a, t in late:
                        if kind == "V":
                            o_root(a, t)
                    late = steps_at(it, s)
                    for kind, a, t in late:
                        if kind == "O":
                            spill(a)
                        if kind == "V" and it == OUT_IT and s == 13:
                            o_root(a, t)
                    if it == OUT_IT and s == 13:
                        late = []
                    if it == OUT_IT and s == 10:
                        pool.wait_ge(gate_out, 64)
                        load_out_operands(0)
                    if it == OUT_IT and s == 15:
                        for u in range(4):
                            wait_free(pool, TURN[("O", OUT_IT - 1, 0)] + u)
                        pool.dma_start(gf_b[:, :], g_final.rearrange("(a d) -> a d", a=1).broadcast_to([P, D_MODEL])
                                       ).then_inc(gf_in, 16)
                    if it > OUT_IT and s == 1:
                        load_out_operands(it - OUT_IT)
            for t in range(TILES):
                pool.wait_ge(y_sq, TILES * (OUTS - 1) + t + 1)
                link(pool.tensor_tensor(ssq[:, t, 0:2], ssq[:, t, 0:2], ssq[:, t, 2:4], ALU.add))
                link(pool.tensor_tensor(ssq[:, t, 0:1], ssq[:, t, 0:1], ssq[:, t, 1:2], ALU.add))
                inv_root(stat[:, 1, t:t + 1], ssq[:, t, 0:1], 1, D_MODEL).then_inc(y_rstd, 1)
            for t in range(TILES):
                pool.wait_ge(y_ready, t + 1)
                dst = y_prompt[0] if t == 0 else y_sample[0, P * (t - 1):P * t, :]
                pool.dma_start(dst, y_sb[:, t, :]).then_inc(y_out, 16)
            pool.wait_ge(state_out, STATE_DONE[OUT_IT - 1])
            for b in range(2):
                pool.wait_ge(row_out[b], 16 * N_SPILL // 2)
            pool.wait_ge(gate_out, 64)
            pool.wait_ge(y_out, 16 * TILES)


_INS = ["x_prompt", "x_sample", "cache_diff_k", "cache_diff_v", "cache_gqa_k", "cache_gqa_v", "c", "c_ctx", "w_ada",
        "b_ada", "g_norm", "w_in", "lam_q1", "lam_k1", "lam_q2", "lam_k2", "subln_g", "q_norm_g", "k_norm_g",
        "w_out", "g_final"]
_OUTS = [(1, P, D_MODEL), (1, LAT * P, D_MODEL), (1, 1, P, H_A, DH), (1, 1, P, H_A, DH), (1, 1, P, KV_B, DH),
         (1, 1, P, KV_B, DH)]


def rope_table(rot_dim):
    n = LAT * P
    token = np.arange(n)
    quarter = rot_dim // 4
    inv_freq = (1.0 / (np.float32(10000.0) ** (np.arange(quarter, dtype=np.float32) / np.float32(quarter)))).astype(np.float32)
    rows = (token // GRID_W).astype(np.float32)[:, None] * inv_freq
    cols = (token % GRID_W).astype(np.float32)[:, None] * inv_freq
    ang = np.concatenate([rows, cols], axis=-1)
    tab = np.stack([np.cos(ang), np.sin(ang)]).astype(np.float32).reshape(2, LAT, P, rot_dim // 2)
    return np.ascontiguousarray(tab.transpose(2, 0, 1, 3))


def kernel(**inputs):
    import concourse.bacc as _bacc
    from concourse.bass_utils import run_bass_kernel_spmd as _run

    nc = _bacc.Bacc("TRN2", target_bir_lowering=False, num_devices=1)
    arrays, args = {}, []
    for name in _INS:
        arrays[f"in_{name}_dram"] = np.ascontiguousarray(inputs[name])
    arrays["ropes_a_dram"] = rope_table(DK_A)
    arrays["ropes_b_dram"] = rope_table(DH)
    for name, a in arrays.items():
        args.append(nc.dram_tensor(name, a.shape, mybir.dt.from_np(a.dtype), kind="ExternalInput").ap())
    for i, shape in enumerate(_OUTS):
        args.append(nc.dram_tensor(f"out_{i}_dram", shape, F32, kind="ExternalOutput").ap())
    build(nc, *args)
    r = _run(nc, [arrays], core_ids=[0])
    return tuple(r.results[0][f"out_{i}_dram"] for i in range(len(_OUTS)))
```

```python
import math
from contextlib import ExitStack

import numpy as np

import concourse.bass as bass
from concourse import mybir

F32 = mybir.dt.float32
F32R = mybir.dt.float32r
ALU = mybir.AluOpType
ACT = mybir.ActivationFunctionType
AX_X = mybir.AxisListType.X

P = 128
D_MODEL = 2048
KT = D_MODEL // P
TILES = 5
LAT = 4
PAST = 2
NKEY = (LAT + PAST) * P
H_A, DK_A = 8, 64
H_B, KV_B, DH = 8, 2, 128
NCOL = 512
LAM_INIT = 0.8 - 0.6 * math.exp(0.0)
EPS = 1e-6
GRID_W = 64
A_COLS = 4 * H_A * DH
QB0 = A_COLS
KB0 = QB0 + H_B * DH
GB0 = KB0 + 2 * KV_B * DH

KV_IT = 0
G_IT = 1
D_IT = G_IT + H_B // 2
OUT_IT = D_IT + H_A
OUTS = D_MODEL // NCOL
ITS = OUT_IT + OUTS
RING = 3
W_RING = 4
W_AHEAD = 3
RAW_RING = 2
ADA_RING = 5
GATE_SLOT = KT - 3
GATE_END = 2 * KT - 1
GATE_RING = 8
BLOCKS = KT // 2
MIX = list(range(H_A, H_A + H_B)) + list(range(H_A))
ROW_LAG = 3
N_SPILL = KT - 2

STEPS = {
    1: [("O", -1)], 3: [("QK", 0)], 4: [("S", 0)], 5: [("S", 1)], 6: [("T", 0)], 7: [("S", 2), ("V", 0)],
    8: [("T", 1)], 9: [("S", 3), ("V", 1)], 10: [("T", 2)], 11: [("S", 4), ("V", 2)], 12: [("T", 3)],
    13: [("V", 3)], 14: [("T", 4)], 15: [("V", 4)],
}
LAST_STEPS = dict(STEPS)
LAST_STEPS[10] = [("T", 2), ("S", 4)]
LAST_STEPS[11] = [("V", 2), ("T", 3)]
LAST_STEPS[12] = [("V", 3), ("T", 4)]
LAST_STEPS[13] = [("V", 4)]
LAST_STEPS[14] = [("O", 0)]
LAST_STEPS[15] = []
LAST_PLACES = {11: [1, 3, 4], 12: [2, 3, 4], 13: [3], 14: [3, 4]}


def group_kind(a):
    return "KV" if a == KV_IT else "G" if a < D_IT else "D"


def heads(a):
    return 2 if group_kind(a) == "G" else 1


def steps_at(it, s):
    out = []
    if it > OUT_IT:
        return out
    for kind, t in (LAST_STEPS if it == OUT_IT else STEPS).get(s, []):
        a = it - 1
        if kind == "O":
            a, t = a + t, 0
        if not 0 <= a < OUT_IT or (group_kind(a) == "KV" and kind != "QK"):
            continue
        out.append((kind, a, t))
    return out


def banks_of(kind, a, t):
    g = group_kind(a)
    if kind == "QK":
        return 4 if g == "KV" else 3
    if kind == "S":
        return 4 if t else 2
    if kind == "T":
        return (2 if t else 1) * (2 if g == "G" and t else 1)
    if kind == "O":
        return 2 * heads(a)
    return 1


def parts_of(kind, a, t):
    return heads(a) if kind == "V" else banks_of(kind, a, t)


def v_first(steps):
    return [kind for kind, *_ in steps][:2] == ["V", "T"]


def pieces_at(it, s):
    flat = [(*step, part) for step in steps_at(it, s) for part in range(parts_of(*step))]
    out = [[] for _ in range(TILES)]
    if it == OUT_IT and s in LAST_PLACES:
        for piece, place in zip(flat, LAST_PLACES[s]):
            out[place].append(piece)
        return out
    for i, piece in enumerate(flat):
        if len(flat) > TILES:
            out[i * TILES // len(flat)].append(piece)
        elif piece[0] == "V":
            out[TILES - 1 if s < KT - 1 else 1 + i].append(piece)
        else:
            out[i].append(piece)
    return out


def gate_pieces(s):
    def begin(s):
        return min(max(0, 2 * KT * (s - GATE_SLOT) // (GATE_END - GATE_SLOT)), 2 * KT)
    return range(begin(s), begin(s + 1))


def count_turns():
    first, place, used = {}, [], [0] * RING

    def take(key, banks):
        first[key] = len(place)
        for b in banks:
            place.append((b, used[b]))
            used[b] += 1
    take("VEC", [2])

    def block(c):
        take(("ADA", c), [c % 2])
        take(("COLS", c), [c % 2])
    block(0)
    for kt in range(KT):
        if kt % 2 and kt // 2 + 1 < BLOCKS:
            block(kt // 2 + 1)
        take(("HT", kt), [2, 2])
    take("GATE", [0])
    b = 0
    for it in range(ITS):
        for s in range(KT):
            for step in steps_at(it, s):
                if step[0] == "QK":
                    b = 0
                n = banks_of(*step)
                if step[:2] == ("QK", KV_IT):
                    take(step, [1, 2, 1, 2])
                    continue
                take(step, [(b + i) % RING for i in range(n)])
                b = (b + n) % RING
    return first, place


TURN, PLACE = count_turns()


def build(nc, x_prompt, x_sample, cache_diff_k, cache_diff_v, cache_gqa_k, cache_gqa_v, c, c_ctx, w_ada,
          b_ada, g_norm, w_in, lam_q1, lam_k1, lam_q2, lam_k2, subln_g, q_norm_g, k_norm_g, w_out, g_final,
          ropes_a, ropes_b, y_prompt, y_sample, new_dk, new_dv, new_gk, new_gv):
    w_in2 = w_in[0]
    w_out2 = w_out[0]
    w_ada2 = w_ada[0]
    wa_v = w_in2[:, 0:A_COLS].rearrange("(k p) (s h c) -> h p k s c", p=P, s=4, h=H_A)
    w_v = w_in2.rearrange("(k p) n -> p k n", p=P)
    wo_v = w_out2.rearrange("(k p) n -> p k n", p=P)
    ada_v = w_ada2.rearrange("(k p) n -> k p n", p=P)
    ada_b = w_ada2[:, 0:2 * D_MODEL].rearrange("(q k p) (u c n) -> c q u p k n", k=4, p=P, u=2, n=2 * P)
    xs_v = x_sample[0].rearrange("(t p) d -> p t d", p=P)
    dk_v = cache_diff_k[0, 0].rearrange("(j p) h d -> p j h d", p=P)
    dv_v = cache_diff_v[0, 0].rearrange("(j p) h d -> p j h d", p=P)
    gk_v = cache_gqa_k[0, 0].rearrange("(j p) h d -> p j h d", p=P)
    gv_v = cache_gqa_v[0, 0].rearrange("(j p) h d -> p j h d", p=P)
    o_spill = nc.dram_tensor("o_spill", (H_A + H_B, P, TILES * P), F32).ap()
    gate_rows = nc.dram_tensor("gate_rows", (2, D_MODEL), F32).ap()

    at = [(nc.sbuf_base + 31) // 32 * 32]

    def region(nbytes):
        start = at[0]
        at[0] += (nbytes + 31) // 32 * 32
        assert at[0] <= nc.sbuf_usable_end, (at[0], nc.sbuf_usable_end)
        return start

    def place(name, shape, dt, start):
        size = 4 * int(np.prod(shape[1:]))
        return nc.alloc_sbuf_tensor_at(name, list(shape), dt, offset=start), start + size

    def new(name, shape, dt=F32):
        return place(name, shape, dt, region(4 * int(np.prod(shape[1:]))))[0]

    xt_hi = new("xt_hi", [P, KT, TILES * P], F32R)
    xt_lo = new("xt_lo", [P, KT, TILES * P], F32R)
    w_hi = new("w_hi", [P, W_RING, NCOL], F32R)
    w_lo = new("w_lo", [P, W_RING, NCOL], F32R)
    w_raw = new("w_raw", [P, RAW_RING, 2, NCOL])
    r1 = region(4 * 12800)
    ada_raw, e = place("ada_raw", [P, ADA_RING, 4, 2, 2 * P], F32, r1)
    lam_raw, e = place("lam_raw", [P, 4, H_A * DK_A], F32, e)
    vec_rows, e = place("vec_rows", [96, P], F32, e)
    cs_t, e = place("cs_t", [P, 32], F32, e)
    q_hi, e = place("q_hi", [P, 2, TILES * P], F32R, r1)
    q_lo, e = place("q_lo", [P, 2, TILES * P], F32R, e)
    k_hi, e = place("k_hi", [P, 2, NKEY + P], F32R, e)
    k_lo, e = place("k_lo", [P, 2, NKEY + P], F32R, e)
    v_hl, e = place("v_hl", [P, 2, 7, 2 * DH], F32R, e)
    pt0 = e
    pt_hi, e = place("pt_hi", [P, 2, NKEY], F32R, e)
    pt_lo, e = place("pt_lo", [P, 2, NKEY], F32R, e)
    assert e <= r1 + 4 * 12800
    gate_q, _ = place("gate_q", [P, 2, D_MODEL // 2], F32, r1)
    gate_pt, _ = place("gate_pt", [P, 3, D_MODEL // 2], F32, pt0)
    y_sb, e = place("y_sb", [P, TILES, D_MODEL], F32, r1)
    gf_b, e = place("gf_b", [P, D_MODEL], F32, e)
    r2 = region(4 * TILES * D_MODEL)
    x_sb, e = place("x_sb", [P, TILES, D_MODEL], F32, r2)
    zs, e = place("zs", [P, TILES, NCOL], F32, r2)
    x_add, _ = place("x_add", [P, TILES, NCOL], F32, r2)
    kv_raw, e = place("kv_raw", [P, 2, 2, 2 * DH], F32, e)
    s0 = e
    s_sb, e = place("s_sb", [P, 2, 2, NKEY], F32, e)
    rope_t, _ = place("rope_t", [P, 4, LAT * NCOL // 4], F32, s0)
    sq_k, _ = place("sq_k", [P, TILES, 2 * DH], F32, s0)
    sq_q, _ = place("sq_q", [P, TILES, 2 * DH], F32, pt0)
    gate_sg, _ = place("gate_sg", [P, 3, D_MODEL // 2], F32, e)
    sg, e = place("sg", [P, TILES, 2 * DH], F32, e)
    og, e = place("og", [P, TILES, 2 * DH], F32, e)
    o_sum, e = place("o_sum", [P, 2, 2 * DH], F32, e)
    sq_o, e = place("sq_o", [P, 2, DH], F32, e)
    assert e <= r2 + 4 * TILES * D_MODEL
    y_junk, _ = place("y_junk", [P, NCOL], F32, s0)
    rs0 = region(4 * 2 * TILES * P)
    row_st, _ = place("row_st", [P, 2, TILES * P], F32, rs0)
    gate_b, _ = place("gate_b", [P, 2, NCOL], F32, rs0)
    rope_a = new("rope_a", [P, 2, LAT, DK_A // 2])
    rope_b = new("rope_b", [P, 2, LAT, DH // 2])
    ident = new("ident", [P, P])
    norms = new("norms", [P, 3, DH])
    ada_rows = new("ada_rows", [P, 512])
    vec = new("vec", [P, 96])
    cs = new("cs", [P, 32])
    mod_a = new("mod_a", [P, KT, 2])
    mod_b = new("mod_b", [P, KT, 2])
    lam = new("lam", [P, 4, H_A])
    small = new("small", [P, 6, TILES, 2])
    stat = new("stat", [P, 2, 16])
    half = new("half", [P, 16])
    ssq = new("ssq", [P, TILES, 4])
    gate_raw = [gate_q[:, i] for i in range(2)] + [gate_pt[:, i] for i in range(3)] + [gate_sg[:, i] for i in range(3)]
    nmax, den, rden, fac, ms, rstd = (small[:, i] for i in range(6))

    with ExitStack() as ctx:
        z_ps = ctx.enter_context(nc.psum_tensor("z_ps", [P, TILES, NCOL], F32))
        ring = [ctx.enter_context(nc.psum_tensor(f"ring{b}", [P, 512], F32)) for b in range(RING)]

        def sem(name):
            return ctx.enter_context(nc.semaphore(name))

        x_in = [sem(f"x_in{t}") for t in range(TILES)]
        vec_in, lam_in, rope_in, norm_in = sem("vec_in"), sem("lam_in"), sem("rope_in"), sem("norm_in")
        ada_in = [sem(f"ada_in{b}") for b in range(ADA_RING)]
        raw_in = [sem(f"raw_in{b}") for b in range(RAW_RING)]
        ada_used = sem("ada_used")
        id_set = sem("id_set")
        cs_step, cs_ready, mod_ready = sem("cs_step"), sem("cs_ready"), sem("mod_ready")
        x_sq, x_rstd, x_hat = sem("x_sq"), sem("x_rstd"), sem("x_hat")
        h_mod, h_hi, h_lo = sem("h_mod"), sem("h_hi"), sem("h_lo")
        w_hi_done, w_lo_done = sem("w_hi_done"), sem("w_lo_done")
        tile_done, z_full, z_free = sem("tile_done"), sem("z_full"), sem("z_free")
        bank_full = [sem(f"bank_full{b}") for b in range(RING)]
        bank_free = [sem(f"bank_free{b}") for b in range(RING)]
        act_chain, dve_chain, pool_chain = sem("act_chain"), sem("dve_chain"), sem("pool_chain")
        kv_in = sem("kv_in")
        qk_ready = sem("qk_ready")
        qk_hi_done = sem("qk_hi_done")
        v_hi_done, v_lo_done = sem("v_hi_done"), sem("v_lo_done")
        sq_ready, zr_ready, zn_ready = sem("sq_ready"), sem("zr_ready"), sem("zn_ready")
        g_exp, g_one, g_inv, g_ready = sem("g_exp"), sem("g_one"), sem("g_inv"), sem("g_ready")
        max_ready, exp_done, p_ready = sem("max_ready"), sem("exp_done"), sem("p_ready")
        pt_hi_done = sem("pt_hi_done")
        o_part, o_sq, o_rstd, og_ready = sem("o_part"), sem("o_sq"), sem("o_rstd"), sem("og_ready")
        row_out, row_in = ([sem(f"row_{w}{b}") for b in range(2)] for w in ("out", "in"))
        o_hi_done, o_lo_done = sem("o_hi_done"), sem("o_lo_done")
        state_out = sem("state_out")
        lam_ready = sem("lam_ready")
        gate_in = [sem(f"gate_in{b}") for b in range(GATE_RING)]
        gate_used, gate_bias, gate_out = sem("gate_used"), sem("gate_bias"), sem("gate_out")
        gate_b_in, x_add_in, gf_in = sem("gate_b_in"), sem("x_add_in"), sem("gf_in")
        y_add, y_sq, y_weighted, y_rstd = sem("y_add"), sem("y_sq"), sem("y_weighted"), sem("y_rstd")
        y_left, y_right, y_out = sem("y_left"), sem("y_right"), sem("y_out")

        def wait_full(eng, n):
            b, i = PLACE[n]
            eng.wait_ge(bank_full[b], i + 1)

        def wait_free(eng, n):
            b, i = PLACE[n]
            eng.wait_ge(bank_free[b], i + 1)

        def RB(n):
            return ring[PLACE[n][0]]

        def free_sem(n):
            return bank_free[PLACE[n][0]]

        def wait_tile(eng, kg):
            it, s = divmod(kg, KT)
            if s == KT - 1:
                eng.wait_ge(z_full, TILES * (it + 1))
            else:
                eng.wait_ge(tile_done, (KT - 1) * it + s + 1)

        def linker(eng, s):
            n = [0]

            def link(ins):
                n[0] += 1
                ins.then_inc(s, 1)
                eng.wait_ge(s, n[0])
            return link

        def n_step(a, t):
            return TILES * (a - 1) + t

        def attn_groups_before(a):
            return a - 1

        N_VH = [1 if group_kind(a) == "D" else 2 if group_kind(a) == "KV" else 0 for a in range(OUT_IT)]

        def qk_parts(a):
            n = TURN[("QK", a, 0)]
            g = group_kind(a)
            S, C = LAT * P, PAST * P
            if g == "D":
                return [(n, 0, S, q_hi[:, 0, 0:S], q_lo[:, 0, 0:S], True),
                        (n + 1, 0, S, k_hi[:, 0, 0:S], k_lo[:, 0, 0:S], True),
                        (n + 2, 0, C + P, k_hi[:, 0, S:S + C + P], k_lo[:, 0, S:S + C + P], False),
                        (n + 2, C + P, P, q_hi[:, 0, S:S + P], q_lo[:, 0, S:S + P], True)]
            if g == "KV":
                return [(n + c, 0, S, k_hi[:, c, 0:S], k_lo[:, c, 0:S], True) for c in range(2)] + \
                    [(n + 2 + c, 0, C + P, k_hi[:, c, S:S + C + P], k_lo[:, c, S:S + C + P], True) for c in range(2)]
            return [(n + c, 0, S, q_hi[:, c, 0:S], q_lo[:, c, 0:S], True) for c in range(2)] + \
                [(n + 2, P * c, P, q_hi[:, c, S:S + P], q_lo[:, c, S:S + P], c == 1) for c in range(2)]

        QKP = [len(qk_parts(a)) for a in range(OUT_IT)]

        def t_parts(a, t):
            n = TURN[("T", a, t)]
            hs = range(heads(a))
            if t == 0:
                return [(n, c, 0, 1, P * c, c == heads(a) - 1) for c in hs]
            return [(n + 2 * c + j // 4, c, j, m, 0, True) for c in hs for j, m in ((0, 4), (4, 2))]

        PT_BEFORE = {}
        npt = 0
        for it_ in range(ITS):
            for s_ in range(KT):
                for kind_, a_, t_ in steps_at(it_, s_):
                    if kind_ == "T":
                        PT_BEFORE[(a_, t_)] = npt
                        npt += len(t_parts(a_, t_))

        V_DONE, OG_DONE, G_DONE, ROW_DONE = [], [], [], []
        v = o_ = gg = ro = 0
        for a in range(OUT_IT):
            v += 2 * N_VH[a]
            V_DONE.append(v)
            if group_kind(a) != "KV":
                o_ += TILES * heads(a)
                gg += TILES
            OG_DONE.append(o_)
            G_DONE.append(gg)
            ro += heads(a) if group_kind(a) != "KV" else 0
            ROW_DONE.append(ro)

        STATE_DONE = [32 * (1 + max(0, a - D_IT + 1)) for a in range(OUT_IT)]
        KV_LOADED = [32 * (1 + max(0, a - D_IT + 1)) for a in range(OUT_IT)]

        SPILLS = [N_SPILL - H_B // 2, H_B // 2]

        def before(table, a):
            return table[a - 1] if a else 0

        def og_index(a, t, c_):
            return before(OG_DONE, a) + heads(a) * t + c_


        block = ctx.enter_context(nc.Block())

        @block.sync
        def _(sp):
            sp.dma_start(vec_rows[0:16, :], c[0].rearrange("(k q) -> k q", q=P)).then_inc(vec_in, 16)
            sp.dma_start(vec_rows[16:32, :], c_ctx.rearrange("(k q) -> k q", q=P)).then_inc(vec_in, 16)
            sp.dma_start(vec_rows[32:48, :], g_norm[0].rearrange("(k q) -> k q", q=P)).then_inc(vec_in, 16)
            sp.dma_start(vec_rows[48:96, :], b_ada[0].rearrange("(k q) -> k q", q=P)).then_inc(vec_in, 16)

            def load_ada(n):
                m = n - ADA_RING
                if m >= 0 and m % 4 == 3:
                    wait_full(sp, TURN[("ADA", m // 4)])
                elif m >= 0:
                    sp.wait_ge(ada_used, 3 * (m // 4) + m % 4 + 1)
                for u in range(2):
                    sp.dma_start(ada_raw[:, n % ADA_RING, :, u, :], ada_b[n // 4, n % 4, u]
                                 ).then_inc(ada_in[n % ADA_RING], 16)

            def load_w(j):
                it, s = divmod(2 * j, KT)
                if j >= RAW_RING:
                    sp.wait_ge(w_lo_done, 2 * (j - RAW_RING) + 2)
                dst = w_raw[:, j % RAW_RING]
                if D_IT <= it < OUT_IT:
                    for u in range(2):
                        sp.dma_start(dst[:, u, :].rearrange("p (s c) -> p s c", s=4),
                                     wa_v[it - D_IT, :, s + u]).then_inc(raw_in[j % RAW_RING], 16)
                    return
                if it == KV_IT:
                    for u in range(2):
                        sp.dma_start(dst[:, u, :], w_v[:, s + u, KB0:KB0 + NCOL]).then_inc(raw_in[j % RAW_RING], 16)
                elif it < D_IT:
                    for u, c0 in enumerate((QB0, GB0)):
                        c0 += 2 * DH * (it - G_IT)
                        sp.dma_start(dst[:, :, 2 * DH * u:2 * DH * (u + 1)],
                                     w_v[:, s:s + 2, c0:c0 + 2 * DH]).then_inc(raw_in[j % RAW_RING], 16)
                else:
                    c0 = NCOL * (it - OUT_IT)
                    for u in range(2):
                        sp.dma_start(dst[:, u, :], wo_v[:, MIX[s + u], c0:c0 + NCOL]).then_inc(raw_in[j % RAW_RING], 16)

            def load_gate(m):
                if m >= GATE_RING:
                    sp.wait_ge(gate_used, m - GATE_RING + 1)
                elif m == 0:
                    wait_full(sp, TURN[("ADA", BLOCKS - 1)])
                elif m == 5:
                    for u in range(2):
                        wait_full(sp, TURN[("HT", KT - 1)] + u)
                k, u = divmod(m, 2)
                c0 = 2 * D_MODEL + u * (D_MODEL // 2)
                sp.dma_start(gate_raw[m % GATE_RING], ada_v[k, :, c0:c0 + D_MODEL // 2]
                             ).then_inc(gate_in[m % GATE_RING], 16)

            for n in range(4):
                load_ada(n)
            for t in range(TILES):
                src = x_prompt[0] if t == 0 else xs_v[:, t - 1, :]
                sp.dma_start(x_sb[:, t, :], src).then_inc(x_in[t], 16)
            load_ada(4)
            load_w(0)
            load_w(1)
            for n in range(ADA_RING, 4 * BLOCKS):
                load_ada(n)
                if n % 4 == 0 and n // 4 >= 2:
                    load_w(n // 4)
            gates = 0
            for j in range(BLOCKS, ITS * KT // 2):
                load_w(j)
                room = 5 if j == BLOCKS else GATE_RING + gate_pieces(2 * j - 5).stop
                while gates < min(room, 2 * KT):
                    load_gate(gates)
                    gates += 1
            for t in range(TILES):
                dst = y_prompt[0] if t == 0 else y_sample[0, P * (t - 1):P * t, :]
                left = NCOL * (OUTS - 1)
                sp.wait_ge(y_left, t + 1)
                sp.dma_start(dst[:, 0:left], y_sb[:, t, 0:left]).then_inc(y_out, 16)
                sp.wait_ge(y_right, t + 1)
                sp.dma_start(dst[:, left:], y_sb[:, t, left:]).then_inc(y_out, 16)
            sp.wait_ge(y_out, 32 * TILES)

        @block.tensor
        def _(pe):
            def claim(n):
                b, i = PLACE[n]
                if i:
                    pe.wait_ge(bank_free[b], i)
                return ring[b]

            def filled(ins, n):
                ins.then_inc(bank_full[PLACE[n][0]], 1)

            def split_matmul(out, hi_l, lo_l, hi_r, lo_r, start=True, stop=True):
                pe.matmul(out, hi_l, hi_r, start=start, stop=False)
                pe.matmul(out, hi_l, lo_r, start=False, stop=False)
                return pe.matmul(out, lo_l, hi_r, start=False, stop=stop)

            pe.wait_ge(id_set, 2)
            pe.wait_ge(vec_in, 64)
            n = TURN["VEC"]
            filled(pe.transpose(claim(n)[:, 0:96], vec_rows[:, :], ident[0:96, 0:96]), n)
            pe.wait_ge(cs_ready, 1)
            csv = cs[:, :].rearrange("p (r k) -> p k r", r=2)

            def modulation(c_, quarter):
                m = 4 * c_ + quarter
                n = TURN[("ADA", c_)]
                bank = claim(n) if quarter == 0 else RB(n)
                pe.wait_ge(ada_in[m % ADA_RING], 32 * (m // ADA_RING + 1))
                for k in range(4):
                    for j in range(4):
                        ins = pe.matmul(bank[32 * j:32 * j + 2, 0:P], csv[:, 4 * quarter + k, :],
                                        ada_raw[:, m % ADA_RING, k, 1 - j // 2, P * (j % 2):P * (j % 2 + 1)],
                                        start=(quarter == 0 and k == 0), stop=(quarter == 3 and k == 3))
                if quarter < 3:
                    ins.then_inc(ada_used, 1)
                else:
                    filled(ins, n)

            def columns(c_):
                n = TURN[("COLS", c_)]
                wait_free(pe, TURN[("ADA", c_)])
                filled(pe.transpose(claim(n)[:, 0:P], ada_rows[:, 0:P], ident[:, :]), n)

            def h_transpose(kt, u):
                n = TURN[("HT", kt)] + u
                bank = claim(n)
                for i, t in enumerate(range(1, TILES) if u == 0 else [0]):
                    if kt == 0 and u == 0:
                        pe.wait_ge(x_hat, t + 1)
                    ins = pe.transpose(bank[:, P * i:P * (i + 1)], x_sb[:, t, P * kt:P * (kt + 1)], ident[:, :])
                filled(ins, n)

            def input_pieces(s, t):
                if s < 2:
                    pieces = {(0, 1): [(1, 1)], (0, 2): [(1, 2)], (0, 4): [(1, 3)],
                              (1, 0): [(2, 0)], (1, 1): [(2, 1)], (1, 3): [(2, 2)]}.get((s, t), [])
                elif s % 2 == 0:
                    pieces = {1: [(s // 2 + 1, 3)], 3: [(s // 2 + 2, 0)]}.get(t, [])
                else:
                    pieces = {1: [(s // 2 + 2, 1)], 3: [(s // 2 + 2, 2)]}.get(t, [])
                done = {(1, 0): 1}.get((s, t)) if s < 2 else s // 2 + 1 if t == 2 and s % 2 == 0 else None
                if done and done < BLOCKS:
                    columns(done)
                for c_, quarter in pieces:
                    if c_ < BLOCKS:
                        modulation(c_, quarter)
                if s + 1 < KT and t in (0, 2):
                    h_transpose(s + 1, t // 2)

            def project_tile(it, s, t):
                b = (it * KT + s) % W_RING
                tok = slice(P * t, P * (t + 1))
                return split_matmul(z_ps[:, t, :], xt_hi[:, s, tok], xt_lo[:, s, tok], w_hi[:, b, :],
                                    w_lo[:, b, :], start=(s == 0), stop=(s == KT - 1))

            def project(it, s, after):
                kg = it * KT + s
                pe.wait_ge(w_lo_done, kg + 1)
                if it == 0:
                    pe.wait_ge(h_lo, s + 1)
                if it == OUT_IT and s < N_SPILL:
                    pe.wait_ge(o_lo_done, s + 1)
                elif it == OUT_IT:
                    for u in range(2):
                        wait_free(pe, TURN[("O", OUT_IT - KT + s, 0)] + u)
                for t in range(TILES):
                    if s == 0 and it:
                        pe.wait_ge(z_free, TILES * (it - 1) + t + 1)
                    ins = project_tile(it, s, t)
                    if s == KT - 1:
                        ins.then_inc(z_full, 1)
                    elif t == TILES - 1:
                        ins.then_inc(tile_done, 1)
                    after(t)

            def transpose(bank, col, src):
                return pe.transpose(bank[:, col:col + P], src, ident[:, :])

            def step_qk(a, part):
                n = TURN[("QK", a, 0)] + part
                g = group_kind(a)
                if part == 0:
                    pe.wait_ge(qk_ready, a + 1)
                    if g != "G":
                        pe.wait_ge(kv_in, KV_LOADED[a])
                bank = claim(n)
                if part < 2:
                    for t in range(1, TILES):
                        ins = transpose(bank, P * (t - 1), zs[:, t, DH * part:DH * (part + 1)])
                elif g == "G":
                    for c_ in range(2):
                        ins = transpose(bank, P * c_, zs[:, 0, DH * c_:DH * (c_ + 1)])
                else:
                    c_ = part - 2 if g == "KV" else 0
                    for j in range(PAST):
                        transpose(bank, P * j, kv_raw[:, 0, j, DH * c_:DH * (c_ + 1)])
                    if g == "KV":
                        ins = transpose(bank, P * PAST, zs[:, 0, DH * c_:DH * (c_ + 1)])
                    else:
                        transpose(bank, P * PAST, zs[:, 0, DH:2 * DH])
                        ins = transpose(bank, P * PAST + P, zs[:, 0, 0:DH])
                filled(ins, n)

            def step_s(a, t, part):
                n = TURN[("S", a, t)] + part
                if t == 0 and part == 0:
                    for u in range(3):
                        wait_free(pe, TURN[("QK", a, 0)] + u)
                if t == 0:
                    c_, k0, kn, q0 = part, NKEY, P, LAT * P
                else:
                    (c_, u), q0 = divmod(part, 2), P * (t - 1)
                    k0, kn = ((0, 512), (512, NKEY - 512))[u]
                if group_kind(a) == "D":
                    rows, qh, kh = slice(DK_A * c_, DK_A * (c_ + 1)), 0, 0
                else:
                    rows, qh, kh = slice(0, P), c_, (a - G_IT) // 2
                filled(split_matmul(claim(n)[:, 0:kn], q_hi[rows, qh, q0:q0 + P], q_lo[rows, qh, q0:q0 + P],
                                    k_hi[rows, kh, k0:k0 + kn], k_lo[rows, kh, k0:k0 + kn]), n)

            def step_t(a, t, part):
                if part == 0:
                    pe.wait_ge(p_ready, n_step(a, t) + 1)
                turn = TURN[("T", a, t)] + part
                bank = claim(turn)
                for n, c_, j0, m, col, _ in t_parts(a, t):
                    for j in range(m if n == turn else 0):
                        ins = transpose(bank, col + P * j, s_sb[:, t % 2, c_, P * (j0 + j):P * (j0 + j + 1)])
                filled(ins, turn)

            def step_v(a, t, c_):
                n = TURN[("V", a, t)]
                if c_ == 0:
                    pe.wait_ge(v_lo_done, V_DONE[a])
                    for m, *_ in t_parts(a, t):
                        wait_free(pe, m)
                bank = claim(n) if c_ == 0 else RB(n)
                tiles = [(0, 0)] if t == 0 else [(j, j + 1) for j in range(LAT + PAST)]
                vh = 0 if group_kind(a) == "D" else (a - G_IT) // 2
                o = 2 * DH * c_
                for j, vt in tiles:
                    keys = slice(P * j, P * (j + 1))
                    pe.matmul(bank[:, o:o + 2 * DH], pt_hi[:, c_, keys], v_hl[:, vh, vt, :],
                              start=(j == 0), stop=False, skip_group_check=True)
                    ins = pe.matmul(bank[:, o:o + DH], pt_lo[:, c_, keys], v_hl[:, vh, vt, 0:DH],
                                    start=False, stop=(j == tiles[-1][0]), skip_group_check=True)
                if c_ == heads(a) - 1:
                    filled(ins, n)

            def step_o(a, part):
                n = TURN[("O", a, 0)] + part
                c_ = part // 2
                d = slice(DH * c_, DH * (c_ + 1))
                if part == 0:
                    pe.wait_ge(og_ready, OG_DONE[a])
                bank = claim(n)
                for i, t in enumerate(range(1, TILES) if part % 2 == 0 else [0]):
                    ins = transpose(bank, P * i, og[:, t, d])
                filled(ins, n)

            def step_gate(s):
                n = TURN["GATE"]
                bank = claim(n) if s == GATE_SLOT else RB(n)
                for m in gate_pieces(s):
                    k, u = divmod(m, 2)
                    pe.wait_ge(gate_in[m % GATE_RING], 16 * (m // GATE_RING + 1))
                    for jj in range(2):
                        j = 2 * u + jj
                        ins = pe.matmul(bank[32 * j:32 * j + 2, :], csv[:, k, :],
                                        gate_raw[m % GATE_RING][:, 512 * jj:512 * (jj + 1)],
                                        start=(k == 0), stop=(k == KT - 1))
                    if m < 2 * KT - 1:
                        ins.then_inc(gate_used, 1)
                    else:
                        filled(ins, n)

            for quarter in range(4):
                modulation(0, quarter)
            columns(0)
            h_transpose(0, 0)
            h_transpose(0, 1)
            modulation(1, 0)

            for it in range(ITS):
                for s in range(KT if it < ITS - 1 else KT - W_RING):
                    pieces = pieces_at(it, s)

                    def between(t):
                        if it == 0:
                            input_pieces(s, t)
                        for kind, a, tile, part in pieces[t]:
                            if kind == "QK":
                                step_qk(a, part)
                            elif kind == "S":
                                step_s(a, tile, part)
                            elif kind == "T":
                                step_t(a, tile, part)
                            elif kind == "V":
                                step_v(a, tile, part)
                            else:
                                step_o(a, part)
                    project(it, s, between)
                    if GATE_SLOT <= KT * it + s < GATE_END:
                        step_gate(KT * it + s)
            for t in range(TILES):
                for s in range(KT - W_RING, KT):
                    if t == 0:
                        pe.wait_ge(w_lo_done, KT * (ITS - 1) + s + 1)
                    ins = project_tile(ITS - 1, s, t)
                ins.then_inc(z_full, 1)

        @block.scalar
        def _(act):
            link = linker(act, act_chain)

            def copy(out, in_, **kw):
                return act.activation(out, in_, ACT.Copy, **kw)

            wait_free(act, TURN["VEC"])
            act.activation(cs_t[:, :], vec[:, 0:32], ACT.Exp, scale=-1.0).then_inc(cs_step, 1)
            for t in range(TILES):
                act.wait_ge(x_in[t], 16)
                if t:
                    act.wait_ge(x_sq, t)
                act.activation(z_ps[:, 0:4, :], x_sb[:, t, :].rearrange("p (b n) -> p b n", b=4), ACT.Square,
                               accum_out=stat[:, 0, t:t + 1]).then_inc(x_sq, 1)

            def modulate(kt):
                if kt % 2 == 0:
                    act.wait_ge(mod_ready, kt // 2 + 1)
                n = TURN[("HT", kt)]
                if kt >= 2:
                    act.wait_ge(h_lo, kt - 1)
                wait_full(act, n)
                act.activation(row_st[:, kt % 2, P:], RB(n)[:, 0:LAT * P], ACT.Identity,
                               bias=mod_b[:, kt, 0:1], scale=mod_a[:, kt, 0:1]).then_inc(free_sem(n), 1)
                n += 1
                wait_full(act, n)
                act.activation(row_st[:, kt % 2, 0:P], RB(n)[:, 0:P], ACT.Identity,
                               bias=mod_b[:, kt, 1:2], scale=mod_a[:, kt, 1:2]).then_inc(free_sem(n), 1)

            def split_w(kg):
                j = kg // 2
                act.wait_ge(raw_in[j % RAW_RING], 32 * (j // RAW_RING + 1))
                if kg >= W_RING:
                    wait_tile(act, kg - W_RING)
                copy(w_hi[:, kg % W_RING, :], w_raw[:, j % RAW_RING, kg % 2, :]).then_inc(w_hi_done, 1)

            def zs_free(it):
                if it:
                    act.wait_ge(qk_ready, it)
                    act.wait_ge(v_lo_done, V_DONE[it - 1])
                    act.wait_ge(g_ready, G_DONE[it - 1])
                    act.wait_ge(state_out, STATE_DONE[it - 1])
                    wait_free(act, TURN[("QK", it - 1, 0)] + banks_of("QK", it - 1, 0) - 1)

            def z_out(it, t):
                act.wait_ge(z_full, TILES * it + t + 1)
                copy(zs[:, t, :], z_ps[:, t, :]).then_inc(z_free, 1)

            def v_hi(a):
                g = group_kind(a)
                if g == "G":
                    return
                act.wait_ge(z_free, TILES * (a + 1))
                for c_ in range(N_VH[a]):
                    v0 = (2 * DH if g == "D" else 2 * DH + DH * c_)
                    copy(v_hl[:, c_, 0:TILES, 0:DH], zs[:, :, v0:v0 + DH]).then_inc(v_hi_done, 1)
                act.wait_ge(kv_in, KV_LOADED[a])
                for c_ in range(N_VH[a]):
                    copy(v_hl[:, c_, TILES:, 0:DH], kv_raw[:, 1, :, DH * c_:DH * (c_ + 1)]).then_inc(v_hi_done, 1)

            def gate_exp(a):
                if group_kind(a) == "KV":
                    return
                act.wait_ge(z_free, TILES * (a + 1))
                act.wait_ge(og_ready, before(OG_DONE, a))
                if a == G_IT:
                    wait_full(act, TURN["GATE"])
                w = DH * heads(a)
                act.activation(sg[:, :, 0:w], zs[:, :, NCOL - w:NCOL], ACT.Exp, scale=-1.0).then_inc(g_exp, 1)

            def qk_his(a):
                for n, col, w, hi, _, _ in qk_parts(a):
                    wait_full(act, n)
                    copy(hi, RB(n)[:, col:col + w]).then_inc(qk_hi_done, 1)

            def scores_out(a, t):
                n = TURN[("S", a, t)]
                if group_kind(a) == "G" and t == 0:
                    act.wait_ge(zr_ready, a + 1)
                parts = [(0, P)] if t == 0 else [(0, 512), (512, 256)]
                for c_ in range(2):
                    for k0, kn in parts:
                        wait_full(act, n)
                        scale = DK_A ** -0.5 if group_kind(a) == "D" else stat[:, 1, 2 * t + c_:2 * t + c_ + 1]
                        copy(s_sb[:, t % 2, c_, k0:k0 + kn], RB(n)[:, 0:kn],
                             scale=scale).then_inc(free_sem(n), 1)
                        n += 1

            def exps(a, t):
                m = n_step(a, t)
                act.wait_ge(max_ready, m + 1)
                kn = NKEY if t else P
                for c_ in range(2):
                    row = s_sb[:, t % 2, c_, 0:kn]
                    act.activation(row, row, ACT.Exp, bias=nmax[:, t, c_:c_ + 1],
                                   accum_out=den[:, t, c_:c_ + 1]).then_inc(exp_done, 1)

            def pt_his(a, t):
                for n, c_, j0, w, col, _ in t_parts(a, t):
                    wait_full(act, n)
                    copy(pt_hi[:, c_, P * j0:P * (j0 + w)], RB(n)[:, col:col + P * w]).then_inc(pt_hi_done, 1)

            def o_low(a, t):
                n = TURN[("V", a, t)]
                m = n_step(a, t)
                act.wait_ge(og_ready, og_index(a, t, 0) - heads(a) if t >= 2 else before(OG_DONE, a))
                wait_full(act, n)
                h = heads(a)
                copy(o_sum[:, t % 2, 0:DH * h].rearrange("p (c d) -> p c d", c=h),
                     RB(n)[:, 0:2 * DH * h].rearrange("p (c u d) -> p c u d", c=h, u=2)[:, :, 1, :]
                     ).then_inc(o_part, 1)

            def o_squares(a, t):
                if group_kind(a) != "D":
                    return
                m = n_step(a, t)
                wait_free(act, TURN[("V", a, t)])
                act.activation(sq_o[:, t % 2, :], o_sum[:, t % 2, 0:DH], ACT.Square, scale=rden[:, t, 0:1],
                               accum_out=ms[:, t, 0:1]).then_inc(o_sq, 1)

            def rows_out(a):
                n = TURN[("O", a, 0)]
                for c_ in range(heads(a)):
                    r = before(ROW_DONE, a) + c_
                    if r < N_SPILL:
                        if a > G_IT:
                            act.wait_ge(row_out[c_], 16 * (a - G_IT))
                        else:
                            act.wait_ge(h_lo, KT)
                        wait_full(act, n)
                        copy(row_st[:, c_, P:], RB(n)[:, 0:LAT * P]).then_inc(free_sem(n), 1)
                        wait_full(act, n + 1)
                        copy(row_st[:, c_, 0:P], RB(n + 1)[:, 0:P]).then_inc(free_sem(n + 1), 1)
                    else:
                        wait_tile(act, KT * OUT_IT - 1)
                        wait_full(act, n)
                        copy(xt_hi[:, r, P:], RB(n)[:, 0:LAT * P]).then_inc(o_hi_done, 1)
                        wait_full(act, n + 1)
                        copy(xt_hi[:, r, 0:P], RB(n + 1)[:, 0:P]).then_inc(o_hi_done, 1)
                    n += 2

            def row_hi(r):
                act.wait_ge(row_in[r % 2], 16 * (r // 2 + 1))
                wait_tile(act, KT * (OUT_IT - 1) + r)
                copy(xt_hi[:, r, :], row_st[:, r % 2, :]).then_inc(o_hi_done, 1)

            def squares(m):
                cc, t = divmod(m, TILES)
                act.wait_ge(y_add, m + 1)
                if m:
                    act.wait_ge(y_sq, m)
                act.activation(y_junk[:, :], y_sb[:, t, NCOL * cc:NCOL * (cc + 1)], ACT.Square,
                               accum_out=ssq[:, t, cc:cc + 1]).then_inc(y_sq, 1)

            def final_scale(t):
                cols = y_sb[:, t, 0:NCOL * (OUTS - 1)]
                act.wait_ge(y_rstd, t + 1)
                if t == 0:
                    act.wait_ge(y_weighted, OUTS - 1)
                copy(cols, cols, scale=stat[:, 1, t:t + 1]).then_inc(y_left, 1)

            modulate(0)
            for kg in range(W_AHEAD):
                split_w(kg)
            late = []
            for it in range(ITS):
                for s in range(KT):
                    old, late = late, steps_at(it, s)
                    kg = it * KT + s + W_AHEAD
                    if s == 0 and 0 < it <= OUT_IT:
                        z_out(it - 1, TILES - 1)
                    if kg < ITS * KT:
                        split_w(kg)
                    if it == 0 and s + 1 < KT:
                        modulate(s + 1)
                    if it == 0 and s == 3:
                        act.wait_ge(lam_ready, 1)
                        act.activation(lam[:, 2:4, :], lam[:, 0:2, :], ACT.Exp).then_inc(lam_ready, 1)
                    if s == 1 and 0 < it <= OUT_IT:
                        v_hi(it - 1)
                        gate_exp(it - 1)
                    if v_first(late):
                        o_low(*late[0][1:])
                    for kind, a, t in late:
                        if kind == "T":
                            pt_his(a, t)
                    for kind, a, t in old:
                        if kind == "S":
                            exps(a, t)
                        if kind == "V":
                            o_squares(a, t)
                    for kind, a, t in late:
                        if kind == "QK":
                            qk_his(a)
                        elif kind == "S":
                            scores_out(a, t)
                    if it < OUT_IT and s == KT - 1:
                        zs_free(it)
                        for t in range(2):
                            z_out(it, t)
                    for kind, a, t in late:
                        if kind == "V":
                            if not v_first(late):
                                o_low(a, t)
                            if a and t == TILES - 1:
                                o_squares(a, t)
                        elif kind == "O":
                            rows_out(a)
                    if it < OUT_IT and s == KT - 1:
                        for t in range(2, TILES - 1):
                            z_out(it, t)
                    late = [step for step in late if step[0] != "V" or step[2] < TILES - 1]
                    r = KT * (it - OUT_IT + 1) + s - ROW_LAG
                    if 0 <= r < N_SPILL:
                        row_hi(r)
                    if it > OUT_IT and s < TILES:
                        squares(TILES * (it - OUT_IT - 1) + s)
            for t in range(TILES):
                squares(TILES * (OUTS - 1) + t)
                if t:
                    final_scale(t - 1)
            final_scale(TILES - 1)

        @block.vector
        def _(dve):
            link = linker(dve, dve_chain)
            link(dve.memset(ada_rows[:, :], 0.0))
            n = TURN["VEC"]
            wait_full(dve, n)
            dve.tensor_copy(vec[:, :], RB(n)[:, 0:96]).then_inc(free_sem(n), 1)
            wait_free(dve, n)
            dve.wait_ge(cs_step, 1)
            link(dve.tensor_scalar(cs[:, :], cs_t[:, :], 1.0, None, ALU.add))
            link(dve.reciprocal(cs_t[:, :], cs[:, :]))
            dve.tensor_tensor(cs[:, :], vec[:, 0:32], cs_t[:, :], ALU.mult).then_inc(cs_ready, 1)
            def modulation_rows(c_):
                n = TURN[("ADA", c_)]
                wait_full(dve, n)
                for j in range(4):
                    rows = slice(32 * j, 32 * j + 2)
                    ins = dve.tensor_copy(ada_rows[rows, 0:P], RB(n)[rows, 0:P])
                ins.then_inc(free_sem(n), 1)

            def modulation_columns(c_):
                n = TURN[("COLS", c_)]
                wait_full(dve, n)
                cols = RB(n)[:, 0:P].rearrange("p (j q) -> p j q", j=4)
                kts = slice(2 * c_, 2 * c_ + 2)

                def vec_of(first):
                    return vec[:, first + 2 * c_:first + 2 * c_ + 2].unsqueeze(2).broadcast_to([P, 2, 2])
                link(dve.scalar_tensor_tensor(mod_a[:, kts, :], cols[:, 0:2, 0:2], 1.0, vec_of(48 + KT), ALU.add,
                                              ALU.add))
                dve.tensor_tensor(mod_b[:, kts, :], cols[:, 2:4, 0:2], vec_of(48), ALU.add).then_inc(free_sem(n), 1)
                dve.tensor_tensor(mod_a[:, kts, :], mod_a[:, kts, :], vec_of(32), ALU.mult).then_inc(mod_ready, 1)

            modulation_rows(0)
            modulation_columns(0)
            for t in range(TILES):
                dve.wait_ge(x_rstd, t + 1)
                dve.tensor_scalar(x_sb[:, t, :], x_sb[:, t, :], stat[:, 1, t:t + 1], None, ALU.mult).then_inc(x_hat, 1)

            def minus_lambda():
                dve.wait_ge(lam_in, 64)
                link(dve.tensor_tensor(lam_raw[:, 0:2, :], lam_raw[:, 0:2, :], lam_raw[:, 2:4, :], ALU.mult))
                dve.tensor_reduce(lam[:, 0:2, :], lam_raw[:, 0:2, :].rearrange("p u (h d) -> p u h d", h=H_A), AX_X,
                                  ALU.add).then_inc(lam_ready, 1)
                dve.wait_ge(lam_ready, 2)
                link(dve.tensor_tensor(lam[:, 0, :], lam[:, 3, :], lam[:, 2, :], ALU.subtract))
                link(dve.tensor_scalar(lam[:, 1, :], lam[:, 0, :], -LAM_INIT, None, ALU.add))
                dve.wait_ge(norm_in, 48)
                link(dve.tensor_scalar(norms[:, 0, :], norms[:, 0, :], 1.0 - LAM_INIT, None, ALU.mult))

            def split_h(kt):
                n = TURN[("HT", kt)]
                wait_free(dve, n)
                wait_free(dve, n + 1)
                dve.tensor_copy(xt_hi[:, kt, :], row_st[:, kt % 2, :]).then_inc(h_hi, 1)
                dve.wait_ge(h_hi, kt + 1)
                dve.tensor_tensor(xt_lo[:, kt, :], row_st[:, kt % 2, :], xt_hi[:, kt, :].bitcast(F32),
                                  ALU.subtract).then_inc(h_lo, 1)

            def split_w(kg):
                dve.wait_ge(w_hi_done, kg + 1)
                b = kg % W_RING
                dve.tensor_tensor(w_lo[:, b, :], w_raw[:, kg // 2 % RAW_RING, kg % 2, :], w_hi[:, b, :].bitcast(F32),
                                  ALU.subtract).then_inc(w_lo_done, 1)

            def norm_sums(a):
                dve.wait_ge(z_free, TILES * (a + 1))
                if a == G_IT:
                    wait_full(dve, TURN["GATE"])
                if group_kind(a) != "D":
                    link(dve.tensor_tensor((sq_k if a == KV_IT else sq_q)[:, :, :], zs[:, :, 0:2 * DH], zs[:, :, 0:2 * DH], ALU.mult))

            def norm_reduce(a):
                if group_kind(a) != "D":
                    ss = stat[:, 0, 0:10].rearrange("p (t c) -> p t c", c=2)
                    dve.tensor_reduce(ss, (sq_k if a == KV_IT else sq_q)[:, :, :].rearrange("p t (c d) -> p t c d", c=2), AX_X,
                                      ALU.add).then_inc(sq_ready, 1)

            def rotate(a):
                g = group_kind(a)
                if g != "D":
                    z2 = zs[:, :, 0:2 * DH].rearrange("p t (c d) -> p t c d", c=2)
                    if g == "KV":
                        dve.wait_ge(zr_ready, a + 1)
                        rs = stat[:, 1, 0:10].rearrange("p (t c) -> p t c", c=2)
                        link(dve.tensor_tensor(z2, z2, rs.unsqueeze(3).broadcast_to([P, TILES, 2, DH]), ALU.mult))
                    w = norms[:, 2 if g == "KV" else 1, :]
                    dve.tensor_tensor(z2, z2, w.unsqueeze(1).unsqueeze(1).broadcast_to([P, TILES, 2, DH]),
                                      ALU.mult).then_inc(zn_ready, 1)
                    dve.wait_ge(zn_ready, a + 1)
                ng, half_d, tab = (4, DK_A // 2, rope_a) if g == "D" else (2, DH // 2, rope_b)
                zz = zs[:, 1:, 0:2 * DH].rearrange("p t (g u d) -> p t g u d", g=ng, u=2)
                x1, x2 = zz[:, :, :, 0, :], zz[:, :, :, 1, :]
                cos, sin = (tab[:, u].unsqueeze(2).broadcast_to([P, LAT, ng, half_d]) for u in range(2))
                tmp = [rope_t[:, u, :].rearrange("p (t g d) -> p t g d", t=LAT, g=ng) for u in range(4)]
                dve.wait_ge(rope_in, 32)
                dve.tensor_tensor(tmp[0], x1, cos, ALU.mult)
                dve.tensor_tensor(tmp[1], x2, sin, ALU.mult)
                dve.tensor_tensor(tmp[2], x1, sin, ALU.mult)
                link(dve.tensor_tensor(tmp[3], x2, cos, ALU.mult))
                link(dve.tensor_tensor(x1, tmp[0], tmp[1], ALU.subtract))
                dve.tensor_tensor(x2, tmp[2], tmp[3], ALU.add).then_inc(qk_ready, 1)

            def v_lo(a):
                g = group_kind(a)
                if g == "G":
                    return
                done = V_DONE[a] - 2 * N_VH[a]
                for c_ in range(N_VH[a]):
                    v0 = (2 * DH if g == "D" else 2 * DH + DH * c_)
                    dve.wait_ge(v_hi_done, done + c_ + 1)
                    dve.tensor_tensor(v_hl[:, c_, 0:TILES, DH:], zs[:, :, v0:v0 + DH],
                                      v_hl[:, c_, 0:TILES, 0:DH].bitcast(F32), ALU.subtract).then_inc(v_lo_done, 1)
                for c_ in range(N_VH[a]):
                    dve.wait_ge(v_hi_done, done + N_VH[a] + c_ + 1)
                    dve.tensor_tensor(v_hl[:, c_, TILES:, DH:], kv_raw[:, 1, :, DH * c_:DH * (c_ + 1)],
                                      v_hl[:, c_, TILES:, 0:DH].bitcast(F32), ALU.subtract).then_inc(v_lo_done, 1)

            def gate_inverse(a, t):
                w = DH * heads(a)
                dve.wait_ge(g_one, attn_groups_before(a) + 1)
                dve.reciprocal(sg[:, t, 0:w], sg[:, t, 0:w]).then_inc(g_inv, 1)

            def qk_los(a):
                q0 = sum(QKP[:a])
                turns = [part[0] for part in qk_parts(a)]
                for n, col, w, hi, lo, last in qk_parts(a):
                    dve.wait_ge(qk_hi_done, q0 + max(i for i, m in enumerate(turns) if m == n) + 1)
                    ins = dve.tensor_tensor(lo, RB(n)[:, col:col + w], hi.bitcast(F32), ALU.subtract)
                    if last:
                        ins.then_inc(free_sem(n), 1)

            def score_max(a, t):
                m = n_step(a, t)
                n = TURN[("S", a, t)]
                for u in range(banks_of("S", a, t)):
                    wait_free(dve, n + u)
                dve.tensor_reduce(nmax[:, t, :], s_sb[:, t % 2, :, 0:(NKEY if t else P)], AX_X, ALU.max,
                                  negate=True).then_inc(max_ready, 1)

            def combine(a, t):
                m = n_step(a, t)
                b = t
                dve.wait_ge(exp_done, 2 * m + 2)
                ins = dve.reciprocal(rden[:, b, :], den[:, b, :])
                if group_kind(a) == "G":
                    ins.then_inc(p_ready, 1)
                    return
                link(ins)
                link(dve.tensor_scalar(fac[:, b, 0:1], rden[:, b, 1:2], den[:, b, 0:1], lam[:, 1, a - D_IT:a - D_IT + 1], ALU.mult,
                                       ALU.mult))
                kn = NKEY if t else P
                e1, e2 = s_sb[:, t % 2, 0, 0:kn], s_sb[:, t % 2, 1, 0:kn]
                dve.scalar_tensor_tensor(e1, e2, fac[:, b, 0:1], e1, ALU.mult, ALU.add).then_inc(p_ready, 1)

            def pt_los(a, t):
                turns = [part[0] for part in t_parts(a, t)]
                for n, c_, j0, w, col, last in t_parts(a, t):
                    dve.wait_ge(pt_hi_done, PT_BEFORE[(a, t)] + max(i for i, m in enumerate(turns) if m == n) + 1)
                    keys = slice(P * j0, P * (j0 + w))
                    ins = dve.tensor_tensor(pt_lo[:, c_, keys], RB(n)[:, col:col + P * w],
                                            pt_hi[:, c_, keys].bitcast(F32), ALU.subtract)
                    if last:
                        ins.then_inc(free_sem(n), 1)

            def o_high(a, t):
                n = TURN[("V", a, t)]
                m = n_step(a, t)
                h = heads(a)
                dve.wait_ge(o_part, m + 1)
                o = o_sum[:, t % 2, 0:DH * h].rearrange("p (c d) -> p c d", c=h)
                dve.tensor_tensor(o, RB(n)[:, 0:2 * DH * h].rearrange("p (c u d) -> p c u d", c=h, u=2)[:, :, 0, :],
                                  o, ALU.add).then_inc(free_sem(n), 1)

            def gated(a, t):
                m = n_step(a, t)
                dve.wait_ge(g_ready, before(G_DONE, a) + t + 1)
                if t == 0 and a and group_kind(a - 1) != "KV":
                    wait_full(dve, TURN[("O", a - 1, 0)] + banks_of("O", a - 1, 0) - 1)
                if group_kind(a) == "D":
                    dve.wait_ge(o_rstd, m - n_step(D_IT, 0) + 1)
                    scale = [rstd[:, t, 1:2]]
                else:
                    wait_free(dve, TURN[("V", a, t)])
                    scale = [rden[:, t, c_:c_ + 1] for c_ in range(2)]
                for c_ in range(heads(a)):
                    d = slice(DH * c_, DH * (c_ + 1))
                    dve.scalar_tensor_tensor(og[:, t, d], o_sum[:, t % 2, d], scale[c_], sg[:, t, d], ALU.mult,
                                             ALU.mult).then_inc(og_ready, 1)

            def rows_lo(a):
                n = TURN[("O", a, 0)]
                for c_ in range(heads(a)):
                    r = before(ROW_DONE, a) + c_
                    if r >= N_SPILL:
                        for u, tok in enumerate((slice(P, None), slice(0, P))):
                            dve.wait_ge(o_hi_done, N_SPILL + 2 * (r - N_SPILL) + u + 1)
                            w = LAT * P if u == 0 else P
                            ins = dve.tensor_tensor(xt_lo[:, r, tok], RB(n + u)[:, 0:w],
                                                    xt_hi[:, r, tok].bitcast(F32), ALU.subtract)
                            ins.then_inc(free_sem(n + u), 1)
                    n += 2

            def row_lo(r):
                dve.wait_ge(o_hi_done, r + 1)
                dve.tensor_tensor(xt_lo[:, r, :], row_st[:, r % 2, :], xt_hi[:, r, :].bitcast(F32),
                                  ALU.subtract).then_inc(o_lo_done, 1)

            def gate_rows_out():
                n = TURN["GATE"]
                dve.wait_ge(gate_bias, 128)
                wait_full(dve, n)
                for j in range(4):
                    rows = slice(32 * j, 32 * j + 2)
                    ins = dve.tensor_tensor(ada_rows[rows, :], RB(n)[rows, :], ada_rows[rows, :], ALU.add)
                ins.then_inc(free_sem(n), 1)

            def gated_y(cc, t):
                dve.wait_ge(z_full, TILES * (OUT_IT + cc) + t + 1)
                cols = y_sb[:, t, NCOL * cc:NCOL * (cc + 1)]
                dve.tensor_tensor(cols, z_ps[:, t, :], gate_b[:, 0 if t else 1, :], ALU.mult).then_inc(z_free, 1)

            def add_x(cc, t):
                cols = y_sb[:, t, NCOL * cc:NCOL * (cc + 1)]
                dve.wait_ge(z_free, TILES * (OUT_IT + cc) + t + 1)
                dve.tensor_tensor(cols, cols, x_add[:, t, :], ALU.add).then_inc(y_add, 1)

            def weight_y(cc):
                dve.wait_ge(gf_in, 16)
                dve.wait_ge(y_sq, TILES * (cc + 1))
                cols = slice(NCOL * cc, NCOL * (cc + 1))
                dve.tensor_tensor(y_sb[:, :, cols], y_sb[:, :, cols],
                                  gf_b[:, cols].unsqueeze(1).broadcast_to([P, TILES, NCOL]),
                                  ALU.mult).then_inc(y_weighted, 1)

            def finish_y(t):
                dve.wait_ge(y_rstd, t + 1)
                cols = slice(NCOL * (OUTS - 1), NCOL * OUTS)
                dve.scalar_tensor_tensor(y_sb[:, t, cols], y_sb[:, t, cols], stat[:, 1, t:t + 1], gf_b[:, cols],
                                         ALU.mult, ALU.mult).then_inc(y_right, 1)

            split_h(0)
            for kg in range(W_AHEAD):
                split_w(kg)
            late = []
            for it in range(ITS):
                for s in range(KT):
                    kg = it * KT + s + W_AHEAD
                    if it > OUT_IT and s == 0:
                        cc = it - OUT_IT - 1
                        dve.wait_ge(gate_b_in, 32 * (cc + 1))
                        dve.wait_ge(x_add_in, 32 * (cc + 1))
                        for t in range(TILES):
                            gated_y(cc, t)
                        for t in range(TILES):
                            add_x(cc, t)
                    if kg < ITS * KT:
                        split_w(kg)
                    if it > OUT_IT and s == TILES + 1:
                        weight_y(it - OUT_IT - 1)
                    if it == 0 and s + 1 < KT:
                        block_done = s % 2 == 0 and s // 2 + 1 < BLOCKS
                        if s == 0:
                            split_h(s + 1)
                        if block_done:
                            modulation_rows(s // 2 + 1)
                        if s:
                            split_h(s + 1)
                        if block_done:
                            modulation_columns(s // 2 + 1)
                    if it == 0 and s == 3:
                        minus_lambda()
                    old, late = late, steps_at(it, s)
                    if v_first(late):
                        o_high(*late[0][1:])
                    for kind, a, t in late:
                        if kind == "T":
                            pt_los(a, t)
                    for kind, a, t in old:
                        if kind == "S":
                            combine(a, t)
                    first = s == 0 or it == OUT_IT and s == KT - 2
                    if first:
                        for kind, a, t in old:
                            if kind == "V":
                                gated(a, t)
                    if 0 < it <= OUT_IT:
                        if s == 0:
                            norm_sums(it - 1)
                            if group_kind(it - 1) == "KV":
                                norm_reduce(it - 1)
                            else:
                                rotate(it - 1)
                        if s == 1 and group_kind(it - 1) == "KV":
                            rotate(it - 1)
                        elif s == 1:
                            norm_reduce(it - 1)
                        if s == 2:
                            v_lo(it - 1)
                        if 4 <= s < 4 + TILES and group_kind(it - 1) != "KV":
                            gate_inverse(it - 1, s - 4)
                    for kind, a, t in late:
                        if kind == "QK":
                            qk_los(a)
                        elif kind == "S":
                            score_max(a, t)
                        elif kind == "V" and not v_first(late):
                            o_high(a, t)
                        elif kind == "O":
                            rows_lo(a)
                    if not first:
                        for kind, a, t in old:
                            if kind == "V":
                                gated(a, t)
                    if it == G_IT + 1 and s == 0:
                        gate_rows_out()
                    r = KT * (it - OUT_IT + 1) + s - ROW_LAG
                    if 0 <= r < N_SPILL:
                        row_lo(r)
            cc = OUTS - 1
            dve.wait_ge(gate_b_in, 32 * (cc + 1))
            dve.wait_ge(x_add_in, 32 * (cc + 1))
            for t in range(TILES):
                gated_y(cc, t)
                add_x(cc, t)
                if t:
                    finish_y(t - 1)
            finish_y(TILES - 1)

        @block.gpsimd
        def _(pool):
            link = linker(pool, pool_chain)
            link(pool.memset(half[:, :], -0.5))
            pool.memset(ident[:, :], 0.0).then_inc(id_set, 1)
            pool.wait_ge(id_set, 1)
            pool.affine_select(out=ident[:, :], in_=ident[:, :], compare_op=ALU.not_equal, fill=1.0, base=0,
                               pattern=[[-1, P]], channel_multiplier=1).then_inc(id_set, 1)
            for i, v_ in enumerate((lam_q1, lam_q2, lam_k1, lam_k2)):
                pool.dma_start(lam_raw[:, i, :], v_.rearrange("a h d -> a (h d)").broadcast_to([P, H_A * DK_A])
                               ).then_inc(lam_in, 16)
            for i, v_ in enumerate((subln_g, q_norm_g, k_norm_g)):
                pool.dma_start(norms[:, i, :], v_.broadcast_to([P, DH])).then_inc(norm_in, 16)
            pool.dma_start(rope_a[:, :, :, :], ropes_a).then_inc(rope_in, 16)
            pool.dma_start(rope_b[:, :, :, :], ropes_b).then_inc(rope_in, 16)

            def inv_root(out, in_, n, mean_of):
                link(pool.tensor_scalar(out, in_, 1.0 / mean_of, EPS, ALU.mult, ALU.add))
                return pool.tensor_tensor(out, out, half[:, 0:n], ALU.pow)

            for t in range(TILES):
                pool.wait_ge(x_sq, t + 1)
                inv_root(stat[:, 1, t:t + 1], stat[:, 0, t:t + 1], 1, D_MODEL).then_inc(x_rstd, 1)

            def load_kv(a):
                g = group_kind(a)
                if g == "G":
                    return
                if a:
                    prev = KV_IT if a == D_IT else a - 1
                    pool.wait_ge(v_lo_done, V_DONE[prev])
                    n = TURN[("QK", prev, 0)]
                    for u in range(banks_of("QK", prev, 0)):
                        wait_free(pool, n + u)
                    pool.wait_ge(kv_in, KV_LOADED[prev])
                else:
                    pool.wait_ge(x_hat, TILES)
                    n = TURN[("HT", KT - 1)]
                    wait_free(pool, n)
                    wait_free(pool, n + 1)
                for u, src in enumerate((dk_v, dv_v) if g == "D" else (gk_v, gv_v)):
                    if g == "D":
                        pool.dma_start(kv_raw[:, u, :, 0:DH], src[:, :, a - D_IT, :]).then_inc(kv_in, 16)
                    else:
                        pool.dma_start(kv_raw[:, u].rearrange("p j (h d) -> p j h d", h=2), src).then_inc(kv_in, 16)

            def state(it):
                g = group_kind(it)
                if g == "D":
                    pool.wait_ge(z_free, TILES * it + 1)
                    pool.dma_start(new_dk[0, 0, :, it - D_IT, :], zs[:, 0, DH:2 * DH]).then_inc(state_out, 16)
                    pool.dma_start(new_dv[0, 0, :, it - D_IT, :], zs[:, 0, 2 * DH:3 * DH]).then_inc(state_out, 16)
                elif g == "KV":
                    pool.wait_ge(zn_ready, 1)
                    pool.dma_start(new_gk[0, 0].rearrange("s h d -> s (h d)"), zs[:, 0, 0:2 * DH]).then_inc(state_out, 16)
                    pool.dma_start(new_gv[0, 0].rearrange("s h d -> s (h d)"), zs[:, 0, 2 * DH:]).then_inc(state_out, 16)

            def gate_one(a):
                pool.wait_ge(g_exp, attn_groups_before(a) + 1)
                w = DH * heads(a)
                pool.tensor_scalar(sg[:, :, 0:w], sg[:, :, 0:w], 1.0, None, ALU.add).then_inc(g_one, 1)

            def gate_mul(a, t):
                w = DH * heads(a)
                pool.wait_ge(g_inv, before(G_DONE, a) + t + 1)
                ins = pool.tensor_tensor(sg[:, t, 0:w], sg[:, t, 0:w], zs[:, t, NCOL - w:NCOL], ALU.mult)
                if group_kind(a) == "D":
                    link(ins)
                    ins = pool.tensor_tensor(sg[:, t, 0:w], sg[:, t, 0:w], norms[:, 0, :], ALU.mult)
                ins.then_inc(g_ready, 1)

            def o_root(a, t):
                if group_kind(a) != "D":
                    return
                pool.wait_ge(o_sq, TILES * (a - D_IT) + t + 1)
                link(inv_root(rstd[:, t, 0:1], ms[:, t, 0:1], 1, DH))
                pool.tensor_tensor(rstd[:, t, 1:2], rstd[:, t, 0:1], rden[:, t, 0:1],
                                   ALU.mult).then_inc(o_rstd, 1)

            def spill(a):
                n = TURN[("O", a, 0)]
                for c_ in range(heads(a)):
                    r = before(ROW_DONE, a) + c_
                    if r < N_SPILL:
                        wait_free(pool, n)
                        wait_free(pool, n + 1)
                        pool.dma_start(o_spill[r], row_st[:, c_, :]).then_inc(row_out[c_], 16)
                    n += 2

            def load_row(r):
                if r < 2:
                    pool.wait_ge(row_out[r], 16 * SPILLS[r])
                else:
                    pool.wait_ge(o_lo_done, r - 1)
                pool.dma_start(row_st[:, r % 2, :], o_spill[r]).then_inc(row_in[r % 2], 16)

            def load_out_operands(cc):
                if cc:
                    pool.wait_ge(y_add, TILES * cc)
                else:
                    pool.wait_ge(state_out, STATE_DONE[OUT_IT - 1])
                    pool.wait_ge(o_lo_done, N_SPILL)
                    pool.wait_ge(g_ready, G_DONE[OUT_IT - 1])
                    wait_free(pool, TURN[("QK", OUT_IT - 1, 0)] + 2)
                cols = slice(NCOL * cc, NCOL * (cc + 1))
                pool.dma_start(x_add[:, 0, :], x_prompt[0, :, cols]).then_inc(x_add_in, 16)
                pool.dma_start(x_add[:, 1:, :], xs_v[:, :, cols]).then_inc(x_add_in, 16)
                for r in range(2):
                    pool.dma_start(gate_b[:, r, :], gate_rows[r:r + 1, cols].broadcast_to([P, NCOL])
                                   ).then_inc(gate_b_in, 16)

            load_kv(0)
            late = []
            for it in range(ITS):
                for s in range(KT):
                    if 0 < it <= OUT_IT:
                        if s == 0 and group_kind(it - 1) == "D":
                            state(it - 1)
                        if s == 0 and it <= D_IT:
                            m = it - 1
                            pool.wait_ge(sq_ready, m + 1)
                            if m == KV_IT:
                                inv_root(stat[:, 1, 0:10], stat[:, 0, 0:10], 10, DH).then_inc(zr_ready, 1)
                            else:
                                link(pool.tensor_scalar(stat[:, 1, 0:10], stat[:, 0, 0:10], DH * EPS, None, ALU.add))
                                pool.tensor_tensor(stat[:, 1, 0:10], stat[:, 1, 0:10], half[:, 0:10],
                                                   ALU.pow).then_inc(zr_ready, 1)
                        if s == 2 and it - 1 == KV_IT:
                            state(it - 1)
                        if s == 1 and group_kind(it - 1) != "KV":
                            gate_one(it - 1)
                        if 4 <= s < 4 + TILES and group_kind(it - 1) != "KV":
                            gate_mul(it - 1, s - 4)
                        if s == 5 and D_IT <= it < OUT_IT:
                            load_kv(it)
                    if it == OUT_IT - 1 and s >= ROW_LAG - 1:
                        load_row(s - (ROW_LAG - 1))
                    if it == G_IT and s == 4:
                        pool.wait_ge(qk_ready, G_IT)
                        for j in range(4):
                            for r in range(2):
                                c0 = 2 * D_MODEL + 512 * j
                                pool.dma_start(ada_rows[32 * j + r:32 * j + r + 1, :], b_ada[:, c0:c0 + 512]
                                               ).then_inc(gate_bias, 16)
                    if it == G_IT + 1 and s == 3:
                        wait_free(pool, TURN["GATE"])
                        for j in range(4):
                            pool.dma_start(gate_rows[:, 512 * j:512 * (j + 1)], ada_rows[32 * j:32 * j + 2, :]
                                           ).then_inc(gate_out, 16)
                    for kind, a, t in late:
                        if kind == "V":
                            o_root(a, t)
                    late = steps_at(it, s)
                    for kind, a, t in late:
                        if kind == "O":
                            spill(a)
                        if kind == "V" and t == TILES - 1:
                            o_root(a, t)
                    late = [step for step in late if step[0] != "V" or step[2] < TILES - 1]
                    if it == OUT_IT and s == 10:
                        pool.wait_ge(gate_out, 64)
                        load_out_operands(0)
                    if it == OUT_IT and s == 15:
                        for u in range(2):
                            wait_free(pool, TURN[("O", OUT_IT - 1, 0)] + u)
                        pool.dma_start(gf_b[:, :], g_final.rearrange("(a d) -> a d", a=1).broadcast_to([P, D_MODEL])
                                       ).then_inc(gf_in, 16)
                    if it > OUT_IT and s == 1:
                        load_out_operands(it - OUT_IT)
            pool.wait_ge(y_sq, TILES * (OUTS - 1))
            for cc in range(1, OUTS - 1):
                link(pool.tensor_tensor(ssq[:, :, 0], ssq[:, :, 0], ssq[:, :, cc], ALU.add))
            link(pool.tensor_scalar(ssq[:, :, 0], ssq[:, :, 0], 1.0 / D_MODEL, EPS, ALU.mult, ALU.add))
            for t in range(TILES):
                pool.wait_ge(y_sq, TILES * (OUTS - 1) + t + 1)
                link(pool.tensor_scalar(stat[:, 1, t:t + 1], ssq[:, t, OUTS - 1:OUTS], 1.0 / D_MODEL, ssq[:, t, 0:1],
                                        ALU.mult, ALU.add))
                pool.tensor_tensor(stat[:, 1, t:t + 1], stat[:, 1, t:t + 1], half[:, 0:1],
                                   ALU.pow).then_inc(y_rstd, 1)
            pool.wait_ge(state_out, STATE_DONE[OUT_IT - 1])
            for b in range(2):
                pool.wait_ge(row_out[b], 16 * SPILLS[b])
            pool.wait_ge(gate_out, 64)


_INS = ["x_prompt", "x_sample", "cache_diff_k", "cache_diff_v", "cache_gqa_k", "cache_gqa_v", "c", "c_ctx", "w_ada",
        "b_ada", "g_norm", "w_in", "lam_q1", "lam_k1", "lam_q2", "lam_k2", "subln_g", "q_norm_g", "k_norm_g",
        "w_out", "g_final"]
_OUTS = [(1, P, D_MODEL), (1, LAT * P, D_MODEL), (1, 1, P, H_A, DH), (1, 1, P, H_A, DH), (1, 1, P, KV_B, DH),
         (1, 1, P, KV_B, DH)]


def rope_table(rot_dim):
    n = LAT * P
    token = np.arange(n)
    quarter = rot_dim // 4
    inv_freq = (1.0 / (np.float32(10000.0) ** (np.arange(quarter, dtype=np.float32) / np.float32(quarter)))).astype(np.float32)
    rows = (token // GRID_W).astype(np.float32)[:, None] * inv_freq
    cols = (token % GRID_W).astype(np.float32)[:, None] * inv_freq
    ang = np.concatenate([rows, cols], axis=-1)
    tab = np.stack([np.cos(ang), np.sin(ang)]).astype(np.float32).reshape(2, LAT, P, rot_dim // 2)
    return np.ascontiguousarray(tab.transpose(2, 0, 1, 3))


def kernel(**inputs):
    import concourse.bacc as _bacc
    from concourse.bass_utils import run_bass_kernel_spmd as _run

    nc = _bacc.Bacc("TRN2", target_bir_lowering=False, num_devices=1)
    arrays, args = {}, []
    for name in _INS:
        arrays[f"in_{name}_dram"] = np.ascontiguousarray(inputs[name])
    arrays["ropes_a_dram"] = rope_table(DK_A)
    arrays["ropes_b_dram"] = rope_table(DH)
    for name, a in arrays.items():
        args.append(nc.dram_tensor(name, a.shape, mybir.dt.from_np(a.dtype), kind="ExternalInput").ap())
    for i, shape in enumerate(_OUTS):
        args.append(nc.dram_tensor(f"out_{i}_dram", shape, F32, kind="ExternalOutput").ap())
    build(nc, *args)
    r = _run(nc, [arrays], core_ids=[0])
    return tuple(r.results[0][f"out_{i}_dram"] for i in range(len(_OUTS)))
```
